# Optimizing a Trainium2 kernel written in Bass

```python
import math
import jax
import jax.numpy as jnp
from jax import lax
import numpy as np

D_MODEL = 2048
BATCH = 1
SEQ = 512
DEPTH = 2
DEC_BATCH = 8
DEC_SEQ = 8
PAST_LEN = 2048
PAGE_SIZE = 128

N_MIXERS = 2
NORM_EPS = 1e-6

DA_HEAD_DIM = 128
DA_V_DIM = 2 * DA_HEAD_DIM
DA_HEADS = D_MODEL // DA_V_DIM
DA_QK_WIDTH = DA_HEADS * 2 * DA_HEAD_DIM
DA_WIDTH = DA_HEADS * DA_V_DIM
DA_LAYER_INDEX = 1
LAMBDA_INIT = 0.8 - 0.6 * math.exp(-0.3 * (DA_LAYER_INDEX - 1))
Q_BLOCK = 128

RET_HEADS = 8
RET_K_DIM = D_MODEL // RET_HEADS
RET_V_DIM = 2 * RET_K_DIM
RET_QK_WIDTH = RET_HEADS * RET_K_DIM
RET_WIDTH = RET_HEADS * RET_V_DIM
RET_CHUNK = 128
ROPE_BASE = 10000.0

kernel_name = 'hybrid_diffattn_retention_step'

def rms_norm(x, w):
    xf = x.astype(jnp.float32)
    y = xf * lax.rsqrt(jnp.mean(xf * xf, axis=-1, keepdims=True) + NORM_EPS)
    return (y * w.astype(jnp.float32)).astype(x.dtype)

def head_rms_norm(x):
    return x * lax.rsqrt(jnp.mean(x * x, axis=-1, keepdims=True) + NORM_EPS)

def alibi_slopes():
    return jnp.exp2(-8.0 * jnp.arange(1, DA_HEADS + 1, dtype=jnp.float32) / DA_HEADS)

def retention_log_decay():
    return jnp.log1p(-jnp.exp2(-5.0 - jnp.arange(RET_HEADS, dtype=jnp.float32)))

def rotate(x, pos):
    half = x.shape[-1] // 2
    inv_freq = 1.0 / (ROPE_BASE ** jnp.linspace(0.0, 1.0, half, dtype=jnp.float32))
    ang = pos.astype(jnp.float32)[:, None] * inv_freq[None, :]
    cos = jnp.cos(ang)[None, :, None, :]
    sin = jnp.sin(ang)[None, :, None, :]
    xf = x.astype(jnp.float32)
    x1, x2 = xf[..., :half], xf[..., half:]
    return jnp.concatenate([x1 * cos - x2 * sin, x1 * sin + x2 * cos], axis=-1)

def diff_lambda(lq1, lk1, lq2, lk2):
    f = jnp.float32
    return (jnp.exp(jnp.sum(lq1.astype(f) * lk1.astype(f)))
            - jnp.exp(jnp.sum(lq2.astype(f) * lk2.astype(f))) + LAMBDA_INIT)

def diff_attn_project(h, w_in):
    b, s, _ = h.shape
    proj = h @ w_in
    q = proj[..., :DA_QK_WIDTH].reshape(b, s, DA_HEADS, 2, DA_HEAD_DIM)
    k = proj[..., DA_QK_WIDTH:2 * DA_QK_WIDTH].reshape(b, s, DA_HEADS, 2, DA_HEAD_DIM)
    v = proj[..., 2 * DA_QK_WIDTH:2 * DA_QK_WIDTH + DA_WIDTH].reshape(b, s, DA_HEADS, DA_V_DIM)
    g = proj[..., 2 * DA_QK_WIDTH + DA_WIDTH:]
    return q, k, v, g

def diff_attn_prompt(q, k, v, lam, slopes):
    b, s, nh, _, d = q.shape
    nb = s // Q_BLOCK
    scale = d ** -0.5
    qb = q.reshape(b, nb, Q_BLOCK, nh, 2, d).transpose(1, 0, 2, 3, 4, 5)
    pos_k = jnp.arange(s, dtype=jnp.int32)

    def block(args):
        q_blk, blk = args
        pos_q = blk * Q_BLOCK + jnp.arange(Q_BLOCK, dtype=jnp.int32)
        dist = (pos_q[:, None] - pos_k[None, :]).astype(jnp.float32)
        sc = jnp.einsum('bqhcd,bkhcd->bchqk', q_blk, k).astype(jnp.float32) * scale
        sc = sc - slopes[:, None, None] * dist[None]
        sc = jnp.where(dist >= 0, sc, -jnp.inf)
        p = jax.nn.softmax(sc, axis=-1)
        p = p[:, 0] - lam * p[:, 1]
        return jnp.einsum('bhqk,bkhe->bqhe', p.astype(v.dtype), v)

    o = lax.map(block, (qb, jnp.arange(nb, dtype=jnp.int32)))
    return o.transpose(1, 0, 2, 3, 4).reshape(b, s, nh, -1)

def diff_attn_sample(q, k_new, v_new, cache_k, cache_v, page_table, lam, slopes):
    db, t, nh, _, d = q.shape
    past = page_table.shape[1] * cache_k.shape[1]
    scale = d ** -0.5
    kp = cache_k[page_table].reshape(db, past, nh, 2, d)
    vp = cache_v[page_table].reshape(db, past, nh, -1)
    pos_q = past + jnp.arange(t, dtype=jnp.int32)
    pos_k = jnp.arange(past + t, dtype=jnp.int32)
    dist = (pos_q[:, None] - pos_k[None, :]).astype(jnp.float32)
    s_past = jnp.einsum('bqhcd,bkhcd->bchqk', q, kp)
    s_new = jnp.einsum('bqhcd,bkhcd->bchqk', q, k_new)
    sc = jnp.concatenate([s_past, s_new], axis=-1).astype(jnp.float32) * scale
    sc = sc - slopes[:, None, None] * dist[None]
    sc = jnp.where(dist >= 0, sc, -jnp.inf)
    p = jax.nn.softmax(sc, axis=-1)
    p = (p[:, 0] - lam * p[:, 1]).astype(v_new.dtype)
    return (jnp.einsum('bhqk,bkhe->bqhe', p[..., :past], vp)
            + jnp.einsum('bhqk,bkhe->bqhe', p[..., past:], v_new))

def diff_attn_output(o, g, subln_w, w_out):
    b, s = o.shape[:2]
    of = head_rms_norm(o.astype(jnp.float32)) * subln_w.astype(jnp.float32) * (1.0 - LAMBDA_INIT)
    gated = of.reshape(b, s, DA_WIDTH).astype(g.dtype) * jax.nn.silu(g)
    return gated @ w_out

def ret_project(h, w_in, pos):
    b, s, _ = h.shape
    proj = h @ w_in
    q = rotate(proj[..., :RET_QK_WIDTH].reshape(b, s, RET_HEADS, RET_K_DIM), pos)
    k = rotate(proj[..., RET_QK_WIDTH:2 * RET_QK_WIDTH].reshape(b, s, RET_HEADS, RET_K_DIM), pos) * (RET_K_DIM ** -0.5)
    v = proj[..., 2 * RET_QK_WIDTH:2 * RET_QK_WIDTH + RET_WIDTH].reshape(b, s, RET_HEADS, RET_V_DIM).astype(jnp.float32)
    g = proj[..., 2 * RET_QK_WIDTH + RET_WIDTH:]
    return q.transpose(0, 2, 1, 3), k.transpose(0, 2, 1, 3), v.transpose(0, 2, 1, 3), g

def retention_chunk(s_prev, q, k, v, log_g):
    c = q.shape[2]
    idx = jnp.arange(c, dtype=jnp.float32)
    diff = idx[:, None] - idx[None, :]
    decay = jnp.where(diff >= 0, jnp.exp(log_g[:, None, None] * jnp.maximum(diff, 0.0)), 0.0)
    scores = jnp.einsum('bhid,bhjd->bhij', q, k) * decay
    o = (jnp.einsum('bhij,bhje->bhie', scores, v)
         + jnp.einsum('bhid,bhde->bhie', q, s_prev) * jnp.exp(log_g[:, None] * (idx + 1.0))[:, :, None])
    k_dec = k * jnp.exp(log_g[:, None] * (c - 1.0 - idx))[:, :, None]
    s_new = jnp.exp(log_g * c)[:, None, None] * s_prev + jnp.einsum('bhjd,bhje->bhde', k_dec, v)
    return s_new, o

def retention_prompt(q, k, v, log_g):
    b, nh, s, dk = q.shape
    dv = v.shape[-1]
    nc = s // RET_CHUNK

    def chunks(t):
        return t.reshape(b, nh, nc, RET_CHUNK, t.shape[-1]).transpose(2, 0, 1, 3, 4)

    def step(state, xs):
        qc, kc, vc = xs
        return retention_chunk(state, qc, kc, vc, log_g)

    s0 = jnp.zeros((b, nh, dk, dv), jnp.float32)
    s_fin, oc = lax.scan(step, s0, (chunks(q), chunks(k), chunks(v)))
    o = oc.transpose(1, 2, 0, 3, 4).reshape(b, nh, s, dv)
    return o, s_fin

def ret_output(o, g, w_out):
    b, _, s, _ = o.shape
    on = head_rms_norm(o).transpose(0, 2, 1, 3).reshape(b, s, RET_WIDTH)
    return (on.astype(g.dtype) * jax.nn.silu(g)) @ w_out

def setup_inputs(seed: int = 0) -> dict:
    key = jax.random.key(seed)
    ks = jax.random.split(key, 20)
    f = jnp.float32
    n_pages = PAST_LEN // PAGE_SIZE
    n_used = DEC_BATCH * n_pages
    n_phys = n_used + (n_used + 3) // 4
    in_attn = 2 * DA_QK_WIDTH + 2 * DA_WIDTH
    in_ret = 2 * RET_QK_WIDTH + 2 * RET_WIDTH

    def gain(k, n):
        return 1.0 + 0.05 * jax.random.normal(k, (n,), f)

    page_table = jax.random.permutation(ks[5], n_phys)[:n_used].reshape(DEC_BATCH, n_pages).astype(jnp.int32)
    return {
        'x_prompt': jax.random.normal(ks[0], (BATCH, SEQ, D_MODEL), f),
        'x_sample': jax.random.normal(ks[1], (DEC_BATCH, DEC_SEQ, D_MODEL), f),
        'cache_k': jax.random.normal(ks[2], (n_phys, PAGE_SIZE, DA_HEADS, 2 * DA_HEAD_DIM), f),
        'cache_v': jax.random.normal(ks[3], (n_phys, PAGE_SIZE, DA_HEADS, DA_V_DIM), f),
        'page_table': page_table,
        'state_ret': 0.5 * jax.random.normal(ks[4], (DEC_BATCH, RET_HEADS, RET_K_DIM, RET_V_DIM), f),
        'norm_pre_attn': gain(ks[6], D_MODEL),
        'w_in_attn': jax.random.normal(ks[7], (D_MODEL, in_attn), f) * D_MODEL ** -0.5,
        'lambda_q1': 0.1 * jax.random.normal(ks[8], (DA_HEAD_DIM,), f),
        'lambda_k1': 0.1 * jax.random.normal(ks[9], (DA_HEAD_DIM,), f),
        'lambda_q2': 0.1 * jax.random.normal(ks[10], (DA_HEAD_DIM,), f),
        'lambda_k2': 0.1 * jax.random.normal(ks[11], (DA_HEAD_DIM,), f),
        'subln_w_attn': gain(ks[12], DA_V_DIM),
        'w_out_attn': jax.random.normal(ks[13], (DA_WIDTH, D_MODEL), f) * DA_WIDTH ** -0.5,
        'norm_post_attn': gain(ks[14], D_MODEL),
        'norm_pre_ret': gain(ks[15], D_MODEL),
        'w_in_ret': jax.random.normal(ks[16], (D_MODEL, in_ret), f) * D_MODEL ** -0.5,
        'w_out_ret': jax.random.normal(ks[17], (RET_WIDTH, D_MODEL), f) * RET_WIDTH ** -0.5,
        'norm_post_ret': gain(ks[18], D_MODEL),
    }

def reference(x_prompt, x_sample, cache_k, cache_v, page_table, state_ret,
              norm_pre_attn, w_in_attn, lambda_q1, lambda_k1, lambda_q2, lambda_k2,
              subln_w_attn, w_out_attn, norm_post_attn,
              norm_pre_ret, w_in_ret, w_out_ret, norm_post_ret):
    slopes = alibi_slopes()
    lam = diff_lambda(lambda_q1, lambda_k1, lambda_q2, lambda_k2)
    log_g = retention_log_decay()
    pos_prompt = jnp.arange(SEQ, dtype=jnp.int32)
    pos_sample = PAST_LEN + jnp.arange(DEC_SEQ, dtype=jnp.int32)
    y_prompt, y_sample = x_prompt, x_sample
    for layer in range(DEPTH):
        if layer % N_MIXERS == 0:
            hp = rms_norm(y_prompt, norm_pre_attn)
            hs = rms_norm(y_sample, norm_pre_attn)
            qp, kp, vp, gp = diff_attn_project(hp, w_in_attn)
            qs, ks_, vs, gs = diff_attn_project(hs, w_in_attn)
            op = diff_attn_prompt(qp, kp, vp, lam, slopes)
            osm = diff_attn_sample(qs, ks_, vs, cache_k, cache_v, page_table, lam, slopes)
            y_prompt = y_prompt + rms_norm(diff_attn_output(op, gp, subln_w_attn, w_out_attn), norm_post_attn)
            y_sample = y_sample + rms_norm(diff_attn_output(osm, gs, subln_w_attn, w_out_attn), norm_post_attn)
            k_prompt = kp.reshape(kp.shape[0], kp.shape[1], DA_HEADS, 2 * DA_HEAD_DIM)
            v_prompt = vp
            k_sample = ks_.reshape(ks_.shape[0], ks_.shape[1], DA_HEADS, 2 * DA_HEAD_DIM)
            v_sample = vs
        else:
            hp = rms_norm(y_prompt, norm_pre_ret)
            hs = rms_norm(y_sample, norm_pre_ret)
            qp, kp, vp, gp = ret_project(hp, w_in_ret, pos_prompt)
            qs, ks_, vs, gs = ret_project(hs, w_in_ret, pos_sample)
            op, sp = retention_prompt(qp, kp, vp, log_g)
            ss, osm = retention_chunk(state_ret.astype(jnp.float32), qs, ks_, vs, log_g)
            y_prompt = y_prompt + rms_norm(ret_output(op, gp, w_out_ret), norm_post_ret)
            y_sample = y_sample + rms_norm(ret_output(osm, gs, w_out_ret), norm_post_ret)
            ret_state_prompt = sp.astype(state_ret.dtype)
            ret_state_sample = ss.astype(state_ret.dtype)
    return (y_prompt, y_sample, k_prompt, v_prompt, ret_state_prompt, k_sample, v_sample, ret_state_sample)


_drawn_inputs = setup_inputs


def setup_inputs(seed=0):
    import zlib

    import numpy as np

    out = dict(_drawn_inputs(seed))
    spreads = {}
    factors = {}
    for name, (base, spread) in spreads.items():
        noise = np.random.default_rng([zlib.crc32(name.encode()), seed]).standard_normal(out[name].shape)
        drawn = base * np.exp(spread * noise) if base else spread * noise
        out[name] = jnp.asarray(drawn.astype(out[name].dtype))
    for name, factor in factors.items():
        out[name] = (out[name] * factor).astype(out[name].dtype)
    return out
```

```python
import concourse.bass as bass
from concourse import mybir
from contextlib import ExitStack
import math
import numpy as np

D = 2048
SEQ = 512
NB, NQ = 8, 8
SMP = NB * NQ
T = SEQ + SMP
HALF = T // 2
PAST, PAGE = 2048, 128
PAGES = PAST // PAGE
HEADS = 8
EPS = 1e-6
LAMBDA_INIT = 0.8 - 0.6 * math.exp(-0.3 * 0)
SCALE = 128 ** -0.5
KT = D // 128
CH = 4
NCH = KT // CH
TILES = [(t, min(128, T - 128 * t)) for t in range(5)]
MASKED = -1e30
HC = 128 + 128 + 64 + 64 + 8 + 1 + 2
RING = 8


def shape_tables():
    slope = 2.0 ** -np.arange(1, 9)
    q, j = np.arange(128)[:, None], np.arange(512)[None]
    dist = q + 384 - j
    bias_prompt = np.stack([np.where(dist >= 0, -s * dist, MASKED) for s in slope])
    pos = np.arange(128)[:, None, None, None, None]
    page = np.arange(PAGES)[None, :, None, None, None]
    tok = np.arange(NQ)[None, None, None, None, :]
    d5 = PAST + tok - 128 * page - pos
    bias_past = np.stack([np.broadcast_to(-slope[2 * g:2 * g + 2].reshape(1, 1, 2, 1, 1) * d5,
                                          (128, PAGES, 2, 2, NQ)).reshape(128, PAGES * 32) for g in range(4)])
    row = np.arange(SMP)
    own = (row[:, None] // NQ == np.arange(NB)[None])[:, :, None, None, None]
    dn = (np.arange(NQ)[None] - (row % NQ)[:, None])[:, None, None, None, :]
    bias_new = np.stack([np.broadcast_to(np.where(own & (dn >= 0), -slope[2 * g:2 * g + 2].reshape(1, 1, 2, 1, 1) * dn, MASKED),
                                         (SMP, NB, 2, 2, NQ)).reshape(SMP, NB * 32) for g in range(4)])
    f = np.float32
    inv = (f(1.0) / (f(10000.0) ** np.linspace(0.0, 1.0, 128, dtype=f))).astype(f)
    where = np.concatenate([np.arange(SEQ), PAST + np.tile(np.arange(NQ), NB)]).astype(f)
    ang = (inv[:, None] * where[None]).astype(f).astype(np.float64)
    rope = np.concatenate([np.cos(ang), np.sin(ang)], 1)
    heads = []
    i = np.arange(128.0)
    for h in range(HEADS):
        lg = math.log1p(-2.0 ** (-5 - h))
        w = 1.0 / 16
        diff = i[None] - i[:, None]
        dec = np.where(diff >= 0, np.exp(lg * np.maximum(diff, 0)), 0) * w
        t = row % NQ
        ds = t[None] - t[:, None]
        decs = np.where((ds >= 0) & (row[None] // NQ == row[:, None] // NQ), np.exp(lg * np.maximum(ds, 0)), 0) * w
        pad = lambda a: np.concatenate([a, np.zeros((128 - a.shape[0], a.shape[1]))])
        rows = lambda a: np.broadcast_to(a[None], (128, a.size))
        kz = np.where(row[:, None] // NQ == np.arange(NB)[None], np.exp(lg * (NQ - 1.0 - t))[:, None], 0) * w
        heads.append(np.concatenate([dec, rows(np.exp(lg * (i + 1))), rows(np.exp(lg * (t + 1.0))), pad(decs), pad(kz),
                                     (np.exp(lg * (127.0 - i)) * w)[:, None],
                                     rows(np.exp(lg * np.array([128.0, 8.0])))], 1))
    eye = np.concatenate([np.eye(128), np.ones((128, 128))], 1)
    return [np.ascontiguousarray(a, dtype=f) for a in (bias_prompt, bias_past, bias_new, rope, np.stack(heads), eye)]


class Stage:
    def __init__(self, kind, /, **a):
        self.kind, self.a, self.upto = kind, a, {}


def adds(s):
    k, a = s.kind, s.a
    if k in ("relay_area", "load_rope", "mask_rows"):
        return {}
    if k == "load_w" or k == "load_g":
        return {f"w_in{a['slot']}": 16}
    if k == "split_w" or k == "split_g":
        return {"w_hi": 1, "w_lo": 1}
    if k == "project":
        i = a["i"]
        return {**({"w_used": 1} if i % 8 == 7 else {}), **({"proj0_full": 1} if i == 27 else {})}
    if k == "evacuate":
        return {f"proj{a['cb']}_drained": 1}
    if k == "rope":
        return {"rotated": 1}
    if k == "norm_tile":
        st = a["stage"]
        out = {"x_in": 16}
        if st:
            out |= {"y_full": 1, "y_drained": 1, "y_var": 1, "y_rstd": 1, "x_sum": 1}
        if st < 2:
            out |= {"x_var": 1, "x_rstd": 1, "x_normed": 1, "xt_full": 1, "x_hi": 1, "x_lo": 1}
        return out
    if k == "store_x":
        return {"x_out": 16}
    table = {
        "load_bias_prompt": {"bias_prompt_in": 16}, "load_bias_sample": {"bias_sample_in": 32},
        "load_head": {"head_in": 16},
        "scores": {"full4": 1, "full5": 1, "drained4": 1, "drained5": 1, "max_ready": 1, "exp_ready": 1, "p_ready": 1},
        "p_transpose": {"full7": 1, "drained7": 1},
        "pv": {"full7": 1, "drained7": 1, "o_var": 1, "o_rstd": 1, "o_normed": 1},
        "o_transpose": {"full7": 1, "drained7": 1},
        "store_gated": {"gated_out": 16},
        "natural": {"full7": 1, "drained7": 1},
        "store_natural": {"natural_out": 32},
        "qk": {"qk_done": 1},
        "soft_new": {"full7": 1, "drained7": 1, "drained6": 1, "pagemax_ready": 1},
        "soft_max": {"full7": 1, "drained7": 1, "diag_ready": 1},
        "soft_exp": {"full7": 1, "drained7": 1, "e_ready": 1, "lsum_ready": 1},
        "soft_len": {"full7": 1, "drained7": 1},
        "value": {"pv_done": 1}, "value_new": {"full6": 1},
        "combine": {"drained6": 1},
        "sample_end": {"sq_ready": 1, "full7": 1, "drained7": 1, "s_rstd": 1, "gs_ready": 1},
        "store_sample": {"gs_out": 16},
        "carry": {"carried": 1},
        "ret_scores": {"full4": 1, "full5": 1, "drained4": 1, "drained5": 1, "qd_ready": 1},
        "ret_out": {"full6": 1, "drained6": 1},
        "ret_state": {"full4": 1, "full5": 1, "drained4": 1, "drained5": 1},
        "store_state_p": {"sp_out": 16},
        "rs_scores": {"full4": 1, "full5": 1, "drained4": 1, "drained5": 1, "qd_ready": 1},
        "rs_intra": {}, "rs_out": {"full6": 1, "drained6": 1},
        "rs_state": {"full4": 1, "full5": 1, "drained4": 1, "drained5": 1},
        "ret_norm": {"o_var": 1, "o_rstd": 1, "o_normed": 1},
    }
    if k in table:
        return table[k]
    if k in ("load_k", "load_v"):
        return {f"{k[-1]}_in{a['p'] % RING}": 16}
    if k == "load_state":
        return {f"state_in{a['b'] % 3}": 16}
    if k == "store_state":
        return {f"state_out{a['b'] % 2}": 16}
    if k == "page":
        n = 4 + a["p"] % 2
        return {f"full{n}": 1, f"drained{n}": 1}
    if k == "gate":
        n = 4 + a["t"] % 2
        return {f"full{n}": 1, f"drained{n}": 1}
    if k == "store_ret":
        return {"gt_out%d" % (a["t"] % 2): 16}
    raise KeyError(k)


class Segment:
    def __init__(self, stages, times=1, first=0):
        self.stages, self.times, self.first = stages, times, first


def project_step(out, i0, w, cols, coef, kinds, inserts, n0, last, krow=0):
    for i in range(32):
        n = n0 * NCH + i // 8
        if i % 8 == 0 and n == 0:
            for m in (0, 1):
                out.append(Stage("load_w", slot=m, **i0(m)))
            out.append(Stage("split_w", slot=0))
            out.append(Stage("load_w", slot=0, **i0(2)))
        for s in inserts.get(i, []):
            out.append(s)
        out.append(Stage("project", i=i))
        if i % 8 == 2 and not (last and i // 8 == NCH - 1):
            out.append(Stage("split_w", slot=(n + 1) % 2))
            if i0(n + 3) is not None:
                out.append(Stage("load_w", slot=(n + 1) % 2, **i0(n + 3)))
        if i == 28:
            out.append(Stage("evacuate", cb=0, **kinds))
    for s in inserts.get(32, []):
        out.append(s)
    out.append(Stage("evacuate", cb=1, **kinds))


def prompt_stages(hp, qb):
    return {0: [Stage("scores", hp=hp, qb=qb)], 12: [Stage("p_transpose", hp=hp, qb=qb)], 14: [Stage("pv", hp=hp, qb=qb)],
            28: [Stage("o_transpose", hp=hp, qb=qb)], 30: [Stage("store_gated", hp=hp, qb=qb)]}


def sample_stages(b):
    at = {}

    def put(i, *s):
        at.setdefault(i, []).extend(s)

    def ahead(kind, p):
        p += RING
        if p < PAGES:
            return [Stage(kind, b=b, p=p)]
        return [Stage(kind, b=b + 1, p=p - PAGES)] if b + 1 < NB else []
    for p in range(PAGES):
        put(2 + p, Stage("page", b=b, p=p), *ahead("load_k", p))
        if p:
            put(2 + p, Stage("qk", b=b, p=p - 1))
    put(18, Stage("qk", b=b, p=PAGES - 1))
    put(18, Stage("soft_new", b=b))
    put(20, Stage("soft_max", b=b))
    put(22, Stage("soft_exp", b=b))
    for p in range(PAGES):
        put(25 + p * 7 // PAGES, Stage("value", b=b, p=p), *ahead("load_v", p))
    put(26, Stage("soft_len", b=b))
    put(32, Stage("value_new", b=b), Stage("combine", b=b))
    return at


def merge(*ds):
    out = {}
    for d in ds:
        for i, s in d.items():
            out.setdefault(i, []).extend(s)
    return out


def attention_pair(first, project, last=False):
    out = []
    if not first:
        out.append(Stage("load_bias_sample"))
        for p in range(RING):
            out += [Stage("load_k", b=0, p=p)]
        for p in range(RING):
            out += [Stage("load_v", b=0, p=p)]

    def chunk(n):
        if n >= 8 * NCH:
            return None
        s, c = divmod(n, NCH)
        return dict(w="in0", row=c * CH, cols=(s % 4) * D + (s // 4) * 256, coef=512)
    for s in range(8):
        hh, kind = divmod(s, 4)
        ins = {}
        if not (first and s < 4) and not (last and s >= 4):
            hp = (hh + 1) % 2
            if kind == 0:
                out.append(Stage("load_bias_prompt", head=hh - 1))
            ins = prompt_stages(hp, kind)
            for i in ins:
                for x in ins[i]:
                    x.a["back"] = hh - 1
        if not first:
            ins = merge(ins, sample_stages(s))
        if project and kind >= 2:
            what = "kv"[kind - 2]
            ins = merge(ins, {3 + 3 * j: [Stage("natural", what=what, hh=hh, j=j)] for j in range(3)},
                        {13: [Stage("store_natural", what=what, hh=hh)]})
        if project:
            project_step(out, chunk, "in0", 0, 0, dict(kind="qkvg"[kind], hh=hh), ins, s, s == 7)
        else:
            for i in range(33):
                out += ins.get(i, [])
    if not first:
        out += [Stage("sample_end"), Stage("store_sample")]
    if project:
        out.append(Stage("carry"))
    return out


def outer_projection(w, krow, add):
    out = []
    for k in range(2):
        out.append(Stage("load_g", slot=k, layer=w, row=krow + k))
    for k in range(KT):
        out.append(Stage("split_g", slot=k % 2, kt=k))
        if k + 2 < KT:
            out.append(Stage("load_g", slot=k % 2, layer=w, row=krow + k + 2))

    def chunk(n):
        if n >= 8 * NCH:
            return None
        s, c = divmod(n, NCH)
        return dict(w=w, row=krow + c * CH, cols=s * 256, coef=0)
    for s in range(8):
        project_step(out, chunk, w, 0, 0, dict(kind="+" if add else "y", hh=s), {}, s, s == 7)
    return out


def retention_head():
    out = [Stage("load_head")] + [Stage("load_state", b=b) for b in range(3)]
    cols = [(0, 256), (D, 256), (2 * D, 512), (2 * D + 256, 512), (4 * D, 512), (4 * D + 256, 512)]
    cols[4], cols[5] = (2 * D + 2 * D, 512), (2 * D + 2 * D + 256, 512)

    def chunk(n):
        if n >= 6 * NCH:
            return None
        s, c = divmod(n, NCH)
        return dict(w="in1", row=c * CH, cols=cols[s][0], coef=cols[s][1])
    for s in range(6):
        ins = {}
        if s in (3, 4):
            ins = merge(ins, {2 + 2 * j: [Stage("natural", what="r", hh=s - 3, j=j)] for j in range(3)})
        if s == 4:
            for c in range(4):
                ins = merge(ins, {8 + 6 * c: [Stage("ret_scores", c=c)], 10 + 6 * c: [Stage("ret_out", c=c)],
                                  12 + 6 * c: [Stage("ret_state", c=c)], min(32, 14 + 6 * c): [Stage("ret_norm", t=c)]})
        if s == 5:
            ins = merge(ins, {0: [Stage("store_state_p"), Stage("rs_scores")], 3: [Stage("rs_intra")]})
            for b in range(NB):
                ins = merge(ins, {4 + 3 * b: [Stage("rs_state", b=b)],
                                  6 + 3 * b: [Stage("store_state", b=b)] + ([Stage("load_state", b=b + 3)] if b + 3 < NB else [])})
            ins = merge(ins, {27: [Stage("rs_out")], 28: [Stage("ret_norm", t=4)]})
        project_step(out, chunk, "in1", 0, 0, dict(kind=["q", "k", "v", "v", "g", "g"][s] + "r", hh=s % 2), ins, s, s == 5)
        if s < 2:
            out.append(Stage("rope", which=s))
    for t in range(5):
        out.append(Stage("gate", t=t))
        out.append(Stage("store_ret", t=t))
    return out


def norm_segment(stage):
    out = []
    for t in range(5):
        out.append(Stage("norm_tile", t=t, stage=stage))
        if stage:
            out.append(Stage("store_x", t=t, stage=stage))
    return out


def plan():
    def relaid(stages):
        return Segment([Stage("relay_area")] + stages)

    segs = [Segment(norm_segment(0)),
            relaid([Stage("mask_rows")] + attention_pair(True, True)),
            Segment(attention_pair(False, True), times=3, first=1),
            Segment(attention_pair(False, False, last=True), first=4),
            relaid(outer_projection("out0", 0, False)),
            Segment(norm_segment(1)),
            relaid([Stage("load_rope")]),
            Segment(retention_head(), times=8),
            relaid(outer_projection("out1", 0, False)),
            Segment(outer_projection("out1", KT, True)),
            Segment(norm_segment(2))]
    names = {}
    for seg in segs:
        total = {}
        for s in seg.stages:
            for name, n in adds(s).items():
                total[name] = total.get(name, 0) + n
                names[name] = n
            s.upto = dict(total)
        seg.total = total
    return segs, sorted(names)


def hybrid_step_kernel(nc, x_prompt, x_sample, cache_k, cache_v, page_table, state_ret, norm_pre_attn, w_in_attn,
                       lambda_q1, lambda_k1, lambda_q2, lambda_k2, subln_w_attn, w_out_attn, norm_post_attn,
                       norm_pre_ret, w_in_ret, w_out_ret, norm_post_ret,
                       y_prompt, y_sample, k_prompt, v_prompt, ret_state_prompt, k_sample, v_sample, ret_state_sample):
    f32, f32r, i32 = mybir.dt.float32, mybir.dt.float32r, mybir.dt.int32
    ALU, ACT, AX = mybir.AluOpType, mybir.ActivationFunctionType, mybir.AxisListType
    MUL, ADD, SUB, MAX = ALU.mult, ALU.add, ALU.subtract, ALU.max

    segs, sem_names = plan()
    bias_prompt_d, bias_past_d, bias_new_d, rope_d, heads_d, eye_d = [
        nc.inline_tensor(a, name=n)[tuple(slice(None) for _ in a.shape)] for a, n in
        zip(shape_tables(), ("bias_prompt", "bias_past", "bias_new", "rope", "ret_heads", "eye"))]
    gated0_d = nc.dram_tensor("gated_attention", (D, T), f32, kind="Internal").ap()
    gated1_d = nc.dram_tensor("gated_retention", (2 * D, T), f32, kind="Internal").ap()
    x1_d = nc.dram_tensor("x_between_layers", (T, D), f32, kind="Internal").ap()

    weights = {"in0": w_in_attn, "in1": w_in_ret, "out0": w_out_attn, "out1": w_out_ret}
    weights = {k: v.rearrange("(k p) n -> p k n", p=128) for k, v in weights.items()}
    gated = {"out0": gated0_d.rearrange("(k p) t -> p k t", p=128), "out1": gated1_d.rearrange("(k p) t -> p k t", p=128)}
    ck = cache_k.rearrange("n s h d -> n s (h d)")
    cv = cache_v.rearrange("n s h d -> n s (h d)")
    xp, xs = x_prompt.rearrange("b s d -> (b s) d"), x_sample.rearrange("b s d -> (b s) d")
    yp, ys = y_prompt.rearrange("b s d -> (b s) d"), y_sample.rearrange("b s d -> (b s) d")
    natural_out = {"k": (k_prompt, k_sample), "v": (v_prompt, v_sample)}
    natural_out = {k: (a.rearrange("b (t p) h d -> p (b t) (h d)", p=128), b.rearrange("b s h d -> (b s) (h d)"))
                   for k, (a, b) in natural_out.items()}
    st_in = state_ret.rearrange("b h (e p) v -> (b h) p e v", p=128)
    st_out = ret_state_sample.rearrange("b h (e p) v -> (b h) p e v", p=128)
    sp_out = ret_state_prompt.rearrange("b h (e p) v -> (b h) p e v", p=128)

    ctx = ExitStack()
    with ctx:
        def sb(name, shape, dt=f32):
            return ctx.enter_context(nc.sbuf_tensor(name, shape, dt))

        XH, XL = sb("XH", [128, KT, T], f32r), sb("XL", [128, KT, T], f32r)
        WR = sb("WR", [128, 2, CH, 256])
        WH, WL = sb("WH", [128, 2, CH, 256], f32r), sb("WL", [128, 2, CH, 256], f32r)
        eye = sb("eye_sb", [128, 256])
        pt = sb("pt", [1, NB * PAGES], i32)
        wpre = sb("wpre", [128, 2, KT])
        subln = sb("subln", [128, 2])
        lam_neg = sb("lam_neg", [128, 1])
        power = sb("power", [128, 128])
        small = sb("small", [128, 8])
        ident, ones = eye[:, 0:128], eye[:, 128:256]
        AREA = 27600
        area = sb("area", [128, AREA])
        used = [0]

        def lay(name, shape, dt=f32):
            n = int(np.prod(shape[1:]))
            lo = used[0]
            used[0] += n
            assert used[0] <= AREA, (name, used[0])
            a = area[0:shape[0], lo:lo + n]
            if dt is not f32:
                a = a.bitcast(dt)
            if len(shape) == 3:
                a = a.rearrange("p (a b) -> p a b", a=shape[1])
            if len(shape) == 4:
                a = a.rearrange("p (a b c) -> p a b c", a=shape[1], b=shape[2])
            return a

        qT, kT = [lay(f"qT{i}", [128, 2, T]) for i in range(2)], [lay(f"kT{i}", [128, 2, T]) for i in range(2)]
        vT, sg = lay("vT", [128, 2, T]), lay("sg", [128, 2, T])
        vn, kn = [lay(f"vn{i}", [128, 5, 256]) for i in range(2)], lay("kn", [128, 5, 256])
        qS, kS, sgN, sgS = [lay(n, [128, 4, SMP]) for n in ("qS", "kS", "sgN", "sgS")]
        vS = lay("vS", [128, 512])
        s_all, e_all = lay("s_all", [128, PAGES + 1, 32]), lay("e_all", [128, PAGES + 1, 32])
        bP, bN = lay("bP", [128, PAGES * 32]), lay("bN", [SMP, NB, 32])
        KTs = lay("KTs", [128, 2, 512])
        oS, oQ = lay("oS", [128, 4, SMP]), lay("oQ", [128, 4, SMP])
        rsS, mx, lp, rl, t64 = lay("rsS", [128, 128]), lay("mx", [128, 32]), lay("lp", [128, 32]), lay("rl", [128, 32]), lay("t64", [128, 64])
        dg, m32 = lay("dg", [32, 32]), lay("m32", [32, 1])
        sc, pT = lay("sc", [128, 2, 512]), lay("pT", [128, 512])
        oP, gP, bH = lay("oP", [128, 256]), lay("gP", [128, 2, 128]), lay("bH", [128, 512])
        junk = lay("junk", [128, 256])
        pst = lay("pst", [128, 8])
        Kr, Vr = lay("Kr", [128, RING, 512]), lay("Vr", [128, RING, 512])
        used[0] = 0
        rope, hc = lay("rope_sb", [128, 2 * T]), lay("hc", [128, HC])
        raw, rqT, rkT = lay("raw", [128, 2, T]), lay("rqT", [128, 2, T]), lay("rkT", [128, 2, T])
        rt = lay("rt", [128, 2, T])
        rvT, rvn, rsg, oN = lay("rvT", [128, 2, T]), lay("rvn", [128, 5, 512]), lay("rsg", [128, 4, T]), lay("oN", [128, 5, 512])
        Sp, Sin, Sout = lay("Sp", [128, 2, 512]), lay("Sin", [128, 3, 1024]), lay("Sout", [128, 2, 1024])
        qd, kd, sT = lay("qd", [128, 2, 128]), lay("kd", [128, 256]), lay("sT", [128, 128])
        qz, kz, gt = lay("qz", [128, 2, T]), lay("kz", [SMP, NB, 256]), lay("gt", [128, 2, 4 * 128])
        rjunk, rst = lay("rjunk", [128, 512]), lay("rst", [128, 4])
        used[0] = 0
        yT = lay("yT", [128, KT, T])
        xt, yn, njunk, wpost = lay("xt", [128, D]), lay("yn", [128, D]), lay("njunk", [128, D]), lay("wpost", [128, D])
        nst = lay("nst", [128, 8])

        bank = [ctx.enter_context(nc.psum_tensor(f"bank{i}", [128, 512], f32)) for i in range(8)]

        sem = {n: ctx.enter_context(nc.semaphore(n)) for n in sem_names}
        const_in = ctx.enter_context(nc.semaphore("const_in"))
        page_table_in = ctx.enter_context(nc.semaphore("page_table_in"))
        wpost_in, wpost_free = ctx.enter_context(nc.semaphore("wpost_in")), ctx.enter_context(nc.semaphore("wpost_free"))
        rope_in = ctx.enter_context(nc.semaphore("rope_in"))
        setup_done = ctx.enter_context(nc.semaphore("setup_done"))
        lam_exp = ctx.enter_context(nc.semaphore("lam_exp"))
        lam_dot = ctx.enter_context(nc.semaphore("lam_dot"))
        starts_done = ctx.enter_context(nc.semaphore("starts_done"))
        sp_passed = ctx.enter_context(nc.semaphore("sp_passed"))
        pe_passed = ctx.enter_context(nc.semaphore("pe_passed"))
        chain_sem = {e: ctx.enter_context(nc.semaphore(f"{e}_order")) for e in ("dve", "act", "pool")}

        def start_of(name):
            return 16 if name.endswith("_out") or "_out" in name else 1

        DMA_NAMES = {n for n in sem_names if "_in" in n or "_out" in n}
        START = {n: (16 if n in DMA_NAMES else 1) for n in sem_names}

        class Count:
            def __init__(self):
                self.start = dict(START)

            def enter(self, seg, i):
                self.seg, self.i = seg, i

            def leave(self):
                for n, v in self.seg.total.items():
                    self.start[n] += v * self.seg.times

            def at(self, stage):
                self.stage, self.own = stage, adds(stage)

            def done(self, name):
                v = self.start[name] + self.stage.upto.get(name, 0)
                if name in self.seg.total and self.seg.times > 1:
                    v = self.i * self.seg.total[name] + v
                return v

            def before(self, name):
                return self.done(name) - self.own.get(name, 0)

        class Order:
            ROOM = 512

            def __init__(self, eng, name):
                self.eng, self.sem, self.start, self.n, self.i = eng, chain_sem[name], 0, 0, None

            def enter(self, seg, i):
                self.seg, self.i, self.n = seg, i, 0

            def leave(self):
                if self.seg.times > 1:
                    assert self.n < self.ROOM, self.n
                    self.eng.nop().then_inc(self.sem, self.ROOM - self.n)
                    self.eng.wait_ge(self.sem, self.start + self.i * self.ROOM + self.ROOM)

            def left(self):
                self.start += self.ROOM * self.seg.times if self.seg.times > 1 else self.n

            def link(self, ins):
                self.n += 1
                ins.then_inc(self.sem, 1)
                v = self.start + self.n
                if self.seg is not None and self.seg.times > 1:
                    v = self.i * self.ROOM + v
                self.eng.wait_ge(self.sem, v)

        def run(eng, cnt, order, do):
            for seg in segs:
                def body(i):
                    cnt.enter(seg, i)
                    if order:
                        order.enter(seg, i)
                    for s in seg.stages:
                        f = do.get(s.kind)
                        if f:
                            cnt.at(s)
                            f(i + seg.first if seg.times > 1 else seg.first, **s.a)
                    if order:
                        order.leave()
                if seg.times > 1:
                    with eng.Fori(0, seg.times) as i:
                        body(i)
                else:
                    body(0)
                cnt.leave()
                if order:
                    order.left()

        def all_done(eng, cnt):
            def f(g):
                for n in cnt.start:
                    if cnt.start[n] > START[n]:
                        eng.wait_ge(sem[n], cnt.start[n])
            return f

        def begin(eng, names, order_sem=None):
            for n in names:
                eng.nop().then_inc(sem[n], START[n])

        PE_NAMES = [n for n in sem_names if n.startswith("full") or n in
                    ("w_used", "proj0_full", "y_full", "xt_full", "qk_done", "pv_done")]
        SP_NAMES = [n for n in sem_names if "_in" in n]
        ACT_NAMES = [n for n in sem_names if "_out" in n] + ["w_hi", "exp_ready", "e_ready", "y_drained", "x_normed", "x_hi",
                                                            "proj0_drained", "proj1_drained"]
        POOL_NAMES = ["o_rstd", "s_rstd", "y_rstd", "x_rstd"]
        DVE_NAMES = [n for n in sem_names if n not in PE_NAMES + SP_NAMES + ACT_NAMES + POOL_NAMES]

        block = ctx.enter_context(nc.Block())

        @block.sync
        def _(sp):
            c = Count()

            begin(sp, SP_NAMES)
            sp.nop().then_inc(starts_done, 1)
            sp.wait_ge(starts_done, 5)
            sp.dma_start(pt[:], page_table.rearrange("b n -> (b n)").unsqueeze(0)).then_inc(page_table_in, 16)
            sp.dma_start(eye[:], eye_d).then_inc(const_in, 16)
            with nc.allow_non_contiguous_dma("small vectors, once"):
                for n, w in enumerate((norm_pre_attn, norm_pre_ret)):
                    sp.dma_start(wpre[:, n, :], w.rearrange("(k p) -> p k", p=128)).then_inc(const_in, 16)
                sp.dma_start(subln[:], subln_w_attn.rearrange("(e p) -> p e", p=128)).then_inc(const_in, 16)
            for n, v in enumerate((lambda_q1, lambda_k1, lambda_q2, lambda_k2)):
                sp.dma_start(njunk[:, n * 128:(n + 1) * 128], v.partition_broadcast(128)).then_inc(const_in, 16)
            sp.wait_ge(page_table_in, 16)

            def stand_apart():
                if c.seg.times > 1:
                    sp.sem_inc(sp_passed, 1)

            def load_w(g, slot, w, row, cols, coef):
                sp.wait_ge(sem["w_lo"], c.before("w_lo"))
                stand_apart()
                col = bass.ds(g * coef + cols, 256) if coef else slice(cols, cols + 256)
                sp.dma_start(WR[:, slot, :, :], weights[w][:, row:row + CH, col]).then_inc(sem[f"w_in{slot}"], 16)

            def load_g(g, slot, layer, row):
                sp.wait_ge(sem["w_lo"], c.before("w_lo"))
                for n in ("gated_out", "gs_out") if layer == "out0" else ("gt_out0", "gt_out1"):
                    sp.wait_ge(sem[n], c.before(n))
                stand_apart()
                sp.dma_start(WR[:, slot, :, :].rearrange("p a b -> p (a b)")[:, 0:T], gated[layer][:, row, :]
                             ).then_inc(sem[f"w_in{slot}"], 16)

            def load_cache(src, ring, name, freed):
                def f(g, b, p):
                    sp.wait_ge(sem[freed(p)], c.before(freed(p)))
                    stand_apart()
                    page = sp.value_load(pt[0:1, b * PAGES + p:b * PAGES + p + 1], min_val=0, max_val=src.shape[0] - 1)
                    sp.dma_start(ring[:, p % RING, :],
                                 src[bass.ds(page, 1), :, bass.ds((g - 1) * 512, 512)].rearrange("a s n -> s (a n)")
                                 ).then_inc(sem[f"{name}_in{p % RING}"], 16)
                return f

            def load_bias_sample(g):
                sp.wait_ge(sem["drained7"], c.before("drained7"))
                sp.wait_ge(sem["drained6"], c.before("drained6"))
                stand_apart()
                sp.dma_start(bP[:], bias_past_d[bass.ds(g - 1, 1), :, :].rearrange("a p n -> p (a n)")).then_inc(sem["bias_sample_in"], 16)
                sp.dma_start(bN[:].rearrange("p a b -> p (a b)"), bias_new_d[bass.ds(g - 1, 1), :, :].rearrange("a p n -> p (a n)")
                             ).then_inc(sem["bias_sample_in"], 16)

            def load_bias_prompt(g, head):
                sp.wait_ge(sem["drained5"], c.before("drained5"))
                stand_apart()
                sp.dma_start(bH[:], bias_prompt_d[bass.ds(g * 2 + head, 1), :, :].rearrange("a p n -> p (a n)")
                             ).then_inc(sem["bias_prompt_in"], 16)

            def load_head(g):
                if True:
                    sp.wait_ge(sem["drained4"], c.before("drained4"))
                    sp.wait_ge(sem["drained5"], c.before("drained5"))
                    sp.wait_ge(sem["drained6"], c.before("drained6"))
                    sp.wait_ge(sem["drained7"], c.before("drained7"))
                stand_apart()
                sp.dma_start(hc[:], heads_d[bass.ds(g, 1), :, :].rearrange("a p n -> p (a n)")).then_inc(sem["head_in"], 16)

            def load_rope(g):
                sp.dma_start(rope[:], rope_d).then_inc(rope_in, 16)

            def load_state(g, b):
                for n in ("full6", "drained4", "drained5", "full5"):
                    sp.wait_ge(sem[n], c.before(n))
                    stand_apart()
                sp.dma_start(Sin[:, b % 3, :].rearrange("p (e v) -> p e v", e=2),
                             st_in[bass.ds(g + b * HEADS, 1), :, :, :].rearrange("a p e v -> p (a e) v")
                             ).then_inc(sem[f"state_in{b % 3}"], 16)

            def norm_tile(g, t, stage):
                R = TILES[t][1]
                if stage and t == 0:
                    sp.wait_ge(sem["proj1_drained"], c.before("proj1_drained"))
                    stand_apart()
                    sp.dma_start(wpost[:], (norm_post_attn, norm_post_ret)[stage - 1].partition_broadcast(128)).then_inc(wpost_in, 16)
                if stage < 2:
                    sp.wait_ge(sem["x_hi"], c.before("x_hi"))
                    sp.wait_ge(sem["x_lo"], c.before("x_lo"))
                sp.wait_ge(sem["x_out"], c.before("x_out"))
                if stage == 0:
                    sp.wait_ge(sem["x_normed"], c.before("x_normed"))
                src = x1_d[t * 128:t * 128 + R, :] if stage == 2 else (xp[t * 128:t * 128 + R, :] if t < 4 else xs)
                sp.dma_start(xt[0:R, :], src).then_inc(sem["x_in"], 16)

            run(sp, c, None, dict(relay_area=all_done(sp, c), load_w=load_w, load_g=load_g, load_k=load_cache(ck, Kr, "k", lambda p: f"full{4 + p % 2}"),
                                  load_v=load_cache(cv, Vr, "v", lambda p: "pv_done"), load_bias_sample=load_bias_sample,
                                  load_bias_prompt=load_bias_prompt, load_head=load_head, load_state=load_state,
                                  norm_tile=norm_tile, load_rope=load_rope))

        @block.tensor
        def _(pe):
            c = Count()

            begin(pe, PE_NAMES)
            pe.nop().then_inc(starts_done, 1)
            pe.wait_ge(starts_done, 5)
            pe.wait_ge(const_in, 8 * 16)
            pe.wait_ge(setup_done, 2)

            def mm(out, a, b, start=True, stop=True):
                return nc.tensor.matmul(out, a, b, start=start, stop=stop, skip_group_check=True)

            def tr(out, a, n=128):
                return nc.tensor.matmul(out, a, ident[0:n, 0:n], start=True, stop=True, is_transpose=True, skip_group_check=True)

            def project(g, i):
                chunk, cb, k = i // 8, (i // 4) % 2, i % 4
                slot, kt = chunk % 2, chunk * CH + k
                if i % 8 == 0:
                    pe.wait_ge(sem["w_lo"], c.before("w_lo"))
                if i == 0:
                    pe.wait_ge(sem["x_lo"], c.before("x_lo"))
                if i in (0, 4):
                    pe.wait_ge(sem[f"proj{cb}_drained"], c.before(f"proj{cb}_drained"))
                w = slice(cb * 128, cb * 128 + 128)
                for n, (a, x) in enumerate(((WH, XH), (WH, XL), (WL, XH))):
                    for half in range(2):
                        last = mm(bank[2 * cb + half][:, 0:HALF], a[:, slot, k, w], x[:, kt, half * HALF:(half + 1) * HALF],
                                  start=kt == 0 and n == 0, stop=kt == KT - 1 and n == 2)
                if i == 27:
                    last.then_inc(sem["proj0_full"], 1)
                elif i % 8 == 7:
                    last.then_inc(sem["w_used"], 1)

            def scores(g, hp, qb, back):
                n = (qb + 1) * 128
                for d in ("proj0_drained", "proj1_drained"):
                    pe.wait_ge(sem[d], c.before(d))
                for cc in range(2):
                    pe.wait_ge(sem[f"drained{4 + cc}"], c.before(f"drained{4 + cc}"))
                    mm(bank[4 + cc][:, 0:n], qT[hp][:, cc, qb * 128:(qb + 1) * 128], kT[hp][:, cc, 0:n]
                       ).then_inc(sem[f"full{4 + cc}"], 1)

            def free7():
                pe.wait_ge(sem["drained7"], c.before("drained7"))

            def p_transpose(g, hp, qb, back):
                pe.wait_ge(sem["p_ready"], c.before("p_ready"))
                free7()
                for k in range(qb + 1):
                    last = tr(bank[7][:, k * 128:(k + 1) * 128], sc[:, 0, k * 128:(k + 1) * 128])
                last.then_inc(sem["full7"], 1)

            def pv(g, hp, qb, back):
                free7()
                for k in range(qb + 1):
                    last = mm(bank[7][:, 0:256], pT[:, k * 128:(k + 1) * 128], vn[hp][:, k, :], start=k == 0, stop=k == qb)
                last.then_inc(sem["full7"], 1)

            def o_transpose(g, hp, qb, back):
                pe.wait_ge(sem["o_normed"], c.before("o_normed"))
                free7()
                for e in range(2):
                    last = tr(bank[7][:, e * 128:(e + 1) * 128], oP[:, e * 128:(e + 1) * 128])
                last.then_inc(sem["full7"], 1)

            def natural(g, what, hh, j):
                for d in ("proj0_drained", "proj1_drained"):
                    pe.wait_ge(sem[d], c.before(d))
                free7()
                if j == 2:
                    pe.sem_inc(pe_passed, 1)
                src = {"k": kT[hh], "v": vT, "r": rvT}[what]
                for t, R in TILES[2 * j:2 * j + 2]:
                    for cb in range(2):
                        o = (t % 2) * 256 + cb * 128
                        last = tr(bank[7][0:R, o:o + 128], src[:, cb, t * 128:t * 128 + R])
                last.then_inc(sem["full7"], 1)

            def page(g, b, p):
                n = 4 + p % 2
                pe.wait_ge(sem[f"k_in{p % RING}"], c.before(f"k_in{p % RING}"))
                pe.wait_ge(sem[f"drained{n}"], c.before(f"drained{n}"))
                for j in range(4):
                    last = tr(bank[n][:, j * 128:(j + 1) * 128], Kr[:, p % RING, j * 128:(j + 1) * 128])
                last.then_inc(sem[f"full{n}"], 1)

            def qk(g, b, p):
                n = 4 + p % 2
                pe.wait_ge(sem[f"drained{n}"], c.before(f"drained{n}"))
                if p == 0:
                    pe.wait_ge(sem["drained6"], c.before("drained6"))
                    pe.wait_ge(sem["carried"], c.before("carried"))
                for j in range(4):
                    last = mm(bank[6][:, p * 32 + j * 8:p * 32 + j * 8 + 8], KTs[:, p % 2, j * 128:(j + 1) * 128],
                              qS[:, j, b * NQ:(b + 1) * NQ])
                last.then_inc(sem["qk_done"], 1)

            def soft_new(g, b):
                free7()
                pe.sem_inc(pe_passed, 1)
                for j in range(4):
                    last = mm(bank[7][0:SMP, j * 8:j * 8 + 8], kS[:, j, :], qS[:, j, b * NQ:(b + 1) * NQ])
                last.then_inc(sem["full7"], 1)

            def soft_max(g, b):
                pe.wait_ge(sem["pagemax_ready"], c.before("pagemax_ready"))
                free7()
                tr(bank[7][0:32, 0:128], mx[:]).then_inc(sem["full7"], 1)

            def soft_exp(g, b):
                pe.wait_ge(sem["diag_ready"], c.before("diag_ready"))
                free7()
                mm(bank[7][:, 0:32], ones[0:32, :], dg[:]).then_inc(sem["full7"], 1)

            def soft_len(g, b):
                pe.wait_ge(sem["lsum_ready"], c.before("lsum_ready"))
                free7()
                mm(bank[7][:, 0:32], ones, lp[:]).then_inc(sem["full7"], 1)

            def value(g, b, p):
                if p == 0:
                    pe.wait_ge(sem["e_ready"], c.before("e_ready"))
                    pe.wait_ge(sem["drained6"], c.before("drained6"))
                pe.wait_ge(sem[f"v_in{p % RING}"], c.before(f"v_in{p % RING}"))
                for j in range(4):
                    hh = j // 2
                    last = mm(bank[6][:, j * 16:(j + 1) * 16], Vr[:, p % RING, j * 128:(j + 1) * 128],
                              e_all[:, p, hh * 16:(hh + 1) * 16], start=p == 0 and j == 0, stop=False)
                last.then_inc(sem["pv_done"], 1)

            def value_new(g, b):
                for j in range(4):
                    hh = j // 2
                    last = mm(bank[6][:, j * 16:(j + 1) * 16], vS[0:SMP, j * 128:(j + 1) * 128],
                              e_all[0:SMP, PAGES, hh * 16:(hh + 1) * 16], start=False, stop=True)
                last.then_inc(sem["full6"], 1)

            def sample_end(g):
                pe.wait_ge(sem["sq_ready"], c.done("sq_ready"))
                free7()
                mm(bank[7][:, 0:256], ones, oQ[:].rearrange("p a b -> p (a b)")).then_inc(sem["full7"], 1)

            def ret_scores(g, c_):
                lo = c_ * 128
                pe.wait_ge(sem["rotated"], c.before("rotated"))
                pe.wait_ge(sem["drained4"], c.before("drained4"))
                for e in range(2):
                    last = mm(bank[4][:, 0:128], rkT[:, e, lo:lo + 128], rqT[:, e, lo:lo + 128], start=e == 0, stop=e == 1)
                last.then_inc(sem["full4"], 1)
                pe.wait_ge(sem["drained5"], c.before("drained5"))
                for e in range(2):
                    last = tr(bank[5][:, e * 128:(e + 1) * 128], rkT[:, e, lo:lo + 128])
                last.then_inc(sem["full5"], 1)

            def ret_out(g, c_):
                for n in ("drained4", "qd_ready", "drained6", "drained7"):
                    pe.wait_ge(sem[n], c.before(n))
                mm(bank[6][:, :], sT[:], rvn[:, c_, :], start=True, stop=c_ == 0)
                if c_ == 0:
                    pe.wait_ge(sem["drained5"], c.before("drained5"))
                last = None
                if c_:
                    for e in range(2):
                        last = mm(bank[6][:, :], qd[:, e, :], Sp[:, e, :], start=False, stop=e == 1)
                    last.then_inc(sem["full6"], 1)

            def ret_out0(g, c_):
                for n in ("drained4", "qd_ready", "drained6", "drained7"):
                    pe.wait_ge(sem[n], c.before(n))
                mm(bank[6][:, :], sT[:], rvn[:, c_, :]).then_inc(sem["full6"], 1)

            def ret_state(g, c_):
                for e in range(2):
                    pe.wait_ge(sem[f"drained{4 + e}"], c.before(f"drained{4 + e}"))
                    if e == 0:
                        pe.wait_ge(sem["drained5"], c.before("drained5"))
                    mm(bank[4 + e][:, :], kd[:, e * 128:(e + 1) * 128], rvn[:, c_, :]).then_inc(sem[f"full{4 + e}"], 1)

            def rs_scores(g):
                pe.wait_ge(sem["drained4"], c.before("drained4"))
                pe.sem_inc(pe_passed, 1)
                for e in range(2):
                    last = mm(bank[4][0:SMP, 0:SMP], rkT[:, e, SEQ:T], rqT[:, e, SEQ:T], start=e == 0, stop=e == 1)
                last.then_inc(sem["full4"], 1)
                pe.wait_ge(sem["drained5"], c.before("drained5"))
                pe.sem_inc(pe_passed, 1)
                for e in range(2):
                    last = tr(bank[5][0:SMP, e * 128:(e + 1) * 128], rkT[:, e, SEQ:T])
                last.then_inc(sem["full5"], 1)

            def rs_intra(g):
                for n in ("drained4", "drained5", "drained6", "qd_ready"):
                    pe.wait_ge(sem[n], c.before(n))
                pe.sem_inc(pe_passed, 1)
                mm(bank[6][0:SMP, :], sT[0:SMP, 0:SMP], rvn[0:SMP, 4, :], start=True, stop=False)

            def rs_state(g, b):
                pe.wait_ge(sem[f"state_in{b % 3}"], c.before(f"state_in{b % 3}"))
                pe.sem_inc(pe_passed, 1)
                for e in range(2):
                    mm(bank[6][0:SMP, :], qz[:, e, b * SMP:(b + 1) * SMP], Sin[:, b % 3, e * 512:(e + 1) * 512],
                       start=False, stop=b == NB - 1 and e == 1)
                for e in range(2):
                    pe.wait_ge(sem[f"drained{4 + e}"], c.before(f"drained{4 + e}"))
                    mm(bank[4 + e][:, :], kz[:, b, e * 128:(e + 1) * 128], rvn[0:SMP, 4, :]).then_inc(sem[f"full{4 + e}"], 1)

            def rs_out(g):
                pe.wait_ge(sem["full5"], c.before("full5"))
                pe.nop().then_inc(sem["full6"], 1)

            def gate(g, t):
                n, R = 4 + t % 2, TILES[t][1]
                if t == 0:
                    pe.wait_ge(sem["o_normed"], c.before("o_normed"))
                pe.wait_ge(sem[f"drained{n}"], c.before(f"drained{n}"))
                pe.sem_inc(pe_passed, 1)
                for j in range(4):
                    last = tr(bank[n][:, j * 128:j * 128 + R], oN[0:R, t, j * 128:(j + 1) * 128], R)
                last.then_inc(sem[f"full{n}"], 1)

            def norm_tile(g, t, stage):
                R = TILES[t][1]
                if stage:
                    for n in ("proj0_drained", "proj1_drained", "x_lo", "y_drained"):
                        pe.wait_ge(sem[n], c.before(n))
                    for j in range(KT):
                        last = tr(bank[j // 4][0:R, (j % 4) * 128:(j % 4) * 128 + 128], yT[:, j, t * 128:t * 128 + R])
                    last.then_inc(sem["y_full"], 1)
                if stage < 2:
                    pe.wait_ge(sem["x_normed"], c.done("x_normed"))
                    if stage:
                        pe.wait_ge(sem["y_drained"], c.done("y_drained"))
                    pe.wait_ge(sem["x_lo"], c.before("x_lo"))
                    for j in range(KT):
                        last = tr(bank[j // 4][:, (j % 4) * 128:(j % 4) * 128 + R], yn[0:R, j * 128:(j + 1) * 128], R)
                    last.then_inc(sem["xt_full"], 1)

            run(pe, c, None, dict(project=project, scores=scores, p_transpose=p_transpose, pv=pv, o_transpose=o_transpose,
                                  natural=natural, page=page, qk=qk, soft_new=soft_new, soft_max=soft_max, soft_exp=soft_exp,
                                  soft_len=soft_len, value=value, value_new=value_new, sample_end=sample_end,
                                  ret_scores=lambda g, c: ret_scores(g, c),
                                  ret_out=lambda g, c: (ret_out if c else ret_out0)(g, c),
                                  ret_state=lambda g, c: ret_state(g, c), rs_scores=rs_scores, rs_intra=rs_intra,
                                  rs_state=rs_state, rs_out=rs_out, gate=gate, norm_tile=norm_tile))

        @block.scalar
        def _(act):
            c, o = Count(), Order(act, "act")

            def copy(out, in_, scale=1.0):
                return nc.scalar.activation(out, in_, ACT.Copy, scale=scale)

            begin(act, ACT_NAMES)
            act.nop().then_inc(starts_done, 1)
            act.wait_ge(starts_done, 5)
            act.wait_ge(lam_dot, 1)
            nc.scalar.activation(small[:, 2:4], small[:, 0:2], ACT.Exp).then_inc(lam_exp, 1)

            def split_w(g, slot):
                act.wait_ge(sem[f"w_in{slot}"], c.before(f"w_in{slot}"))
                act.wait_ge(sem["w_used"], c.before("w_used"))
                copy(WH[:, slot, :, :], WR[:, slot, :, :]).then_inc(sem["w_hi"], 1)
                act.wait_ge(sem["w_hi"], c.done("w_hi"))

            def split_g(g, slot, kt):
                act.wait_ge(sem[f"w_in{slot}"], c.before(f"w_in{slot}"))
                act.wait_ge(sem["w_used"], c.before("w_used"))
                copy(XH[:, kt, :], WR[:, slot, :, :].rearrange("p a b -> p (a b)")[:, 0:T]).then_inc(sem["w_hi"], 1)
                act.wait_ge(sem["w_hi"], c.done("w_hi"))

            def evacuate(g, cb, kind, hh):
                full = "w_used" if cb else "proj0_full"
                act.wait_ge(sem[full], c.before(full))
                if kind == "+":
                    return
                f, extra = ACT.Copy, None
                if kind == "g":
                    act.wait_ge(sem["drained7"], c.before("drained7"))
                    act.wait_ge(sem["carried"], c.before("carried"))
                    dst, f, extra = sg[:, cb, :], ACT.Silu, sgN[:, hh * 2 + cb, :]
                elif kind == "gr":
                    for n in ("drained4", "drained5"):
                        act.wait_ge(sem[n], c.before(n))
                    dst, f = rsg[:, hh * 2 + cb, :], ACT.Silu
                elif kind in ("q", "k"):
                    act.wait_ge(sem["full7"], c.before("full7"))
                    act.wait_ge(sem["carried"], c.before("carried"))
                    act.wait_ge(sem["full4"], c.before("full4"))
                    act.wait_ge(sem["full5"], c.before("full5"))
                    dst = (qT if kind == "q" else kT)[hh][:, cb, :]
                elif kind == "v":
                    act.wait_ge(sem["full7"], c.before("full7"))
                    dst = vT[:, cb, :]
                elif kind in ("qr", "kr"):
                    act.wait_ge(sem["rotated"], c.before("rotated"))
                    dst = raw[:, cb, :]
                elif kind == "vr":
                    act.wait_ge(sem["full7"], c.before("full7"))
                    dst = rvT[:, cb, :]
                else:
                    for n in ("drained4", "drained5", "drained6", "drained7"):
                        act.wait_ge(sem[n], c.before(n))
                    dst = yT[:, hh * 2 + cb, :]
                o.link(nc.scalar.activation(dst[:, 0:HALF], bank[2 * cb][:, 0:HALF], f))
                last = nc.scalar.activation(dst[:, HALF:T], bank[2 * cb + 1][:, 0:HALF], f)
                if extra is not None:
                    o.link(last)
                    last = copy(extra, dst[:, SEQ:T])
                last.then_inc(sem[f"proj{cb}_drained"], 1)
                act.wait_ge(sem[f"proj{cb}_drained"], c.done(f"proj{cb}_drained"))

            def scores(g, hp, qb, back):
                n = (qb + 1) * 128
                act.wait_ge(sem["max_ready"], c.done("max_ready"))
                for cc in range(2):
                    ins = nc.scalar.activation(sc[:, cc, 0:n], sc[:, cc, 0:n], ACT.Exp, bias=pst[:, cc:cc + 1],
                                               accum_out=pst[:, 2 + cc:3 + cc])
                    if cc:
                        ins.then_inc(sem["exp_ready"], 1)
                        act.wait_ge(sem["exp_ready"], c.done("exp_ready"))
                    else:
                        o.link(ins)

            def p_transpose(g, hp, qb, back):
                n = (qb + 1) * 128
                act.wait_ge(sem["full7"], c.done("full7"))
                copy(pT[:, 0:n], bank[7][:, 0:n]).then_inc(sem["drained7"], 1)
                act.wait_ge(sem["drained7"], c.done("drained7"))

            def natural(g, what, hh, j):
                act.wait_ge(sem["full7"], c.done("full7"))
                if what == "r":
                    for n in ("full4", "full5", "full6"):
                        act.wait_ge(sem[n], c.before(n))
                elif j == 0:
                    act.wait_ge(sem["natural_out"], c.before("natural_out"))
                dst = {"k": kn, "v": vn[hh], "r": rvn}[what]
                cols = slice(hh * 256, hh * 256 + 256) if what == "r" else slice(0, 256)
                if j < 2:
                    ins = copy(dst[:, 2 * j:2 * j + 2, cols], bank[7][:, :].rearrange("p (a b) -> p a b", a=2))
                else:
                    ins = copy(dst[0:SMP, 4, cols], bank[7][0:SMP, 0:256])
                ins.then_inc(sem["drained7"], 1)
                act.wait_ge(sem["drained7"], c.done("drained7"))

            def store_natural(g, what, hh):
                src = {"k": kn, "v": vn[hh]}[what]
                dp, ds = natural_out[what]
                col = bass.ds(g * 512 + hh * 256, 256)
                act.dma_start(dp[:, :, col], src[:, 0:4, :]).then_inc(sem["natural_out"], 16)
                act.dma_start(ds[:, col], src[0:SMP, 4, :]).then_inc(sem["natural_out"], 16)

            def store_gated(g, hp, qb, back):
                act.wait_ge(sem["drained7"], c.before("drained7"))
                row = g * 512 + back * 256
                act.dma_start(gated0_d[bass.ds(row, 256), qb * 128:(qb + 1) * 128].rearrange("(e p) t -> p e t", p=128), gP[:]
                              ).then_inc(sem["gated_out"], 16)

            def page(g, b, p):
                if p % 2 == 0:
                    act.wait_ge(sem["full4"], c.done("full4"))
                    act.wait_ge(sem["qk_done"], c.before("qk_done"))
                    copy(KTs[:, 0, :], bank[4][:, :]).then_inc(sem["drained4"], 1)
                    act.wait_ge(sem["drained4"], c.done("drained4"))

            def soft_exp(g, b):
                act.wait_ge(sem["drained7"], c.done("drained7"))
                nc.scalar.activation(e_all[:], e_all[:], ACT.Exp).then_inc(sem["e_ready"], 1)
                act.wait_ge(sem["e_ready"], c.done("e_ready"))

            def store_sample(g):
                act.wait_ge(sem["gs_ready"], c.before("gs_ready"))
                act.dma_start(gated0_d[bass.ds(g * 512 - 512, 512), SEQ:T].rearrange("(k p) t -> p k t", p=128), oQ[:]
                              ).then_inc(sem["gs_out"], 16)

            def ret_scores(g, c_):
                act.wait_ge(sem["full5"], c.done("full5"))
                copy(kd[:], bank[5][:, 0:256], scale=hc[:, 392:393]).then_inc(sem["drained5"], 1)
                act.wait_ge(sem["drained5"], c.done("drained5"))

            def ret_out(g, c_):
                act.wait_ge(sem["full6"], c.done("full6"))
                act.wait_ge(sem["full4"], c.before("full4"))
                copy(oN[:, c_, :], bank[6][:, :]).then_inc(sem["drained6"], 1)
                act.wait_ge(sem["drained6"], c.done("drained6"))

            def rs_out(g):
                act.wait_ge(sem["full6"], c.done("full6"))
                copy(oN[0:SMP, 4, :], bank[6][0:SMP, :]).then_inc(sem["drained6"], 1)
                act.wait_ge(sem["drained6"], c.done("drained6"))

            def store_state_p(g):
                act.wait_ge(sem["drained4"], c.before("drained4"))
                act.wait_ge(sem["drained5"], c.before("drained5"))
                act.dma_start(sp_out[bass.ds(g, 1), :, :, :].rearrange("a p e v -> p (a e) v"), Sp[:]).then_inc(sem["sp_out"], 16)

            def store_state(g, b):
                act.wait_ge(sem["drained4"], c.before("drained4"))
                act.wait_ge(sem["drained5"], c.before("drained5"))
                act.dma_start(st_out[bass.ds(g + b * HEADS, 1), :, :, :].rearrange("a p e v -> p (a e) v"),
                              Sout[:, b % 2, :].rearrange("p (e v) -> p e v", e=2)).then_inc(sem[f"state_out{b % 2}"], 16)

            def store_ret(g, t):
                n, R = 4 + t % 2, TILES[t][1]
                act.wait_ge(sem[f"drained{n}"], c.before(f"drained{n}"))
                act.dma_start(gated1_d[bass.ds(g * 512, 512), t * 128:t * 128 + R].rearrange("(k p) t -> p k t", p=128),
                              gt[:, t % 2, :].rearrange("p (k t) -> p k t", k=4)[:, :, 0:R]).then_inc(sem[f"gt_out{t % 2}"], 16)

            def norm_tile(g, t, stage):
                R = TILES[t][1]
                if stage:
                    act.wait_ge(sem["y_full"], c.done("y_full"))
                    act.wait_ge(sem["x_out"], c.before("x_out"))
                    act.wait_ge(sem["xt_full"], c.before("xt_full"))
                    for j in range(4):
                        ins = copy(yn[0:R, j * 512:(j + 1) * 512], bank[j][0:R, :])
                        if j == 3:
                            ins.then_inc(sem["y_drained"], 1)
                            act.wait_ge(sem["y_drained"], c.done("y_drained"))
                        else:
                            o.link(ins)
                if stage < 2:
                    act.wait_ge(sem["x_rstd"], c.done("x_rstd"))
                    act.wait_ge(sem["xt_full"], c.before("xt_full"))
                    copy(yn[0:R, :], xt[0:R, :], scale=nst[0:R, 3:4]).then_inc(sem["x_normed"], 1)
                    act.wait_ge(sem["x_normed"], c.done("x_normed"))
                    act.wait_ge(sem["xt_full"], c.done("xt_full"))
                    for j in range(KT):
                        ins = copy(XH[:, j, t * 128:t * 128 + R], bank[j // 4][:, (j % 4) * 128:(j % 4) * 128 + R],
                                   scale=wpre[:, stage, j:j + 1])
                        if j == KT - 1:
                            ins.then_inc(sem["x_hi"], 1)
                            act.wait_ge(sem["x_hi"], c.done("x_hi"))
                        else:
                            o.link(ins)

            def store_x(g, t, stage):
                R = TILES[t][1]
                act.wait_ge(sem["x_sum"], c.before("x_sum"))
                dst = x1_d[t * 128:t * 128 + R, :] if stage == 1 else (yp[t * 128:t * 128 + R, :] if t < 4 else ys)
                act.dma_start(dst, xt[0:R, :]).then_inc(sem["x_out"], 16)

            run(act, c, o, dict(relay_area=all_done(act, c), split_w=split_w, split_g=split_g, evacuate=evacuate, scores=scores, p_transpose=p_transpose,
                                natural=natural, store_natural=store_natural, store_gated=store_gated, page=page,
                                soft_exp=soft_exp, store_sample=store_sample,
                                ret_scores=lambda g, c: ret_scores(g, c), ret_out=lambda g, c: ret_out(g, c),
                                rs_out=rs_out, store_state_p=store_state_p, store_state=store_state, store_ret=store_ret,
                                norm_tile=norm_tile, store_x=store_x))
            for n in sem_names:
                if "_out" in n:
                    act.wait_ge(sem[n], c.start[n])

        @block.vector
        def _(dve):
            c, o = Count(), Order(dve, "dve")
            v = nc.vector

            def variance(ss, n):
                return v.tensor_scalar(ss, ss, 1.0 / n, EPS, MUL, ADD)

            begin(dve, DVE_NAMES)
            dve.nop().then_inc(starts_done, 1)
            dve.wait_ge(starts_done, 5)
            o.seg = None
            dve.wait_ge(const_in, 8 * 16)
            for n in range(2):
                o.link(v.tensor_tensor_reduce(out=njunk[:, 512:640], in0=njunk[:, n * 256:n * 256 + 128],
                                              in1=njunk[:, n * 256 + 128:n * 256 + 256], scale=1.0, scalar=0.0, op0=MUL, op1=ADD,
                                              accum_out=small[:, n:n + 1]))
            v.memset(power[:], -0.5).then_inc(lam_dot, 1)
            dve.wait_ge(lam_exp, 1)
            o.link(v.tensor_tensor(lam_neg[:], small[:, 3:4], small[:, 2:3], SUB))
            v.tensor_scalar(lam_neg[:], lam_neg[:], -LAMBDA_INIT, None, ADD).then_inc(setup_done, 1)
            v.tensor_scalar(subln[:], subln[:], 1.0 - LAMBDA_INIT, None, MUL).then_inc(setup_done, 1)
            dve.wait_ge(setup_done, 2)
            o.start = o.n

            def mask_rows(g):
                o.link(v.memset(s_all[:, PAGES, :], MASKED))

            def split_w(g, slot):
                dve.wait_ge(sem["w_hi"], c.done("w_hi"))
                v.tensor_tensor(WL[:, slot, :, :], WR[:, slot, :, :], WH[:, slot, :, :].bitcast(f32), SUB).then_inc(sem["w_lo"], 1)
                dve.wait_ge(sem["w_lo"], c.done("w_lo"))

            def split_g(g, slot, kt):
                dve.wait_ge(sem["w_hi"], c.done("w_hi"))
                v.tensor_tensor(XL[:, kt, :], WR[:, slot, :, :].rearrange("p a b -> p (a b)")[:, 0:T],
                                XH[:, kt, :].bitcast(f32), SUB).then_inc(sem["w_lo"], 1)
                dve.wait_ge(sem["w_lo"], c.done("w_lo"))

            def evacuate(g, cb, kind, hh):
                if kind == "+":
                    full = "w_used" if cb else "proj0_full"
                    dve.wait_ge(sem[full], c.before(full))
                    dst = yT[:, hh * 2 + cb, :]
                    o.link(v.tensor_tensor(dst[:, 0:HALF], bank[2 * cb][:, 0:HALF], dst[:, 0:HALF], ADD))
                    v.tensor_tensor(dst[:, HALF:T], bank[2 * cb + 1][:, 0:HALF], dst[:, HALF:T], ADD).then_inc(sem[f"proj{cb}_drained"], 1)
                    dve.wait_ge(sem[f"proj{cb}_drained"], c.done(f"proj{cb}_drained"))

            def scores(g, hp, qb, back):
                n = (qb + 1) * 128
                dve.wait_ge(sem["bias_prompt_in"], c.before("bias_prompt_in"))
                dve.wait_ge(sem["full7"], c.before("full7"))
                for cc in range(2):
                    dve.wait_ge(sem[f"full{4 + cc}"], c.done(f"full{4 + cc}"))
                    v.scalar_tensor_tensor(out=sc[:, cc, 0:n], in0=bank[4 + cc][:, 0:n], scalar=SCALE,
                                           in1=bH[:, 384 - qb * 128:512], op0=MUL, op1=ADD).then_inc(sem[f"drained{4 + cc}"], 1)
                    dve.wait_ge(sem[f"drained{4 + cc}"], c.done(f"drained{4 + cc}"))
                for cc in range(2):
                    ins = v.reduce_max(pst[:, cc:cc + 1], sc[:, cc, 0:n], AX.X, negate=True)
                    if cc:
                        ins.then_inc(sem["max_ready"], 1)
                        dve.wait_ge(sem["max_ready"], c.done("max_ready"))
                    else:
                        o.link(ins)
                dve.wait_ge(sem["exp_ready"], c.done("exp_ready"))
                o.link(v.reciprocal(pst[:, 4:6], pst[:, 2:4]))
                o.link(v.tensor_scalar(pst[:, 5:6], pst[:, 5:6], lam_neg[:], None, MUL))
                o.link(v.tensor_scalar(sc[:, 0, 0:n], sc[:, 0, 0:n], pst[:, 4:5], None, MUL))
                v.scalar_tensor_tensor(out=sc[:, 0, 0:n], in0=sc[:, 1, 0:n], scalar=pst[:, 5:6], in1=sc[:, 0, 0:n],
                                       op0=MUL, op1=ADD).then_inc(sem["p_ready"], 1)
                dve.wait_ge(sem["p_ready"], c.done("p_ready"))

            def pv(g, hp, qb, back):
                dve.wait_ge(sem["full7"], c.done("full7"))
                v.tensor_copy(oP[:], bank[7][:, 0:256]).then_inc(sem["drained7"], 1)
                dve.wait_ge(sem["drained7"], c.done("drained7"))
                o.link(v.tensor_tensor_reduce(out=junk[:], in0=oP[:], in1=oP[:], scale=1.0, scalar=0.0, op0=MUL, op1=ADD,
                                              accum_out=pst[:, 6:7]))
                variance(pst[:, 6:7], 256).then_inc(sem["o_var"], 1)
                dve.wait_ge(sem["o_var"], c.done("o_var"))
                dve.wait_ge(sem["o_rstd"], c.done("o_rstd"))
                v.tensor_scalar(oP[:], oP[:], pst[:, 7:8], None, MUL).then_inc(sem["o_normed"], 1)
                dve.wait_ge(sem["o_normed"], c.done("o_normed"))

            def o_transpose(g, hp, qb, back):
                dve.wait_ge(sem["full7"], c.done("full7"))
                dve.wait_ge(sem["proj0_drained"], c.before("proj0_drained"))
                dve.wait_ge(sem["proj1_drained"], c.before("proj1_drained"))
                dve.wait_ge(sem["gated_out"], c.before("gated_out"))
                for e in range(2):
                    ins = v.scalar_tensor_tensor(out=gP[:, e, :], in0=bank[7][:, e * 128:(e + 1) * 128], scalar=subln[:, e:e + 1],
                                                 in1=sg[:, e, qb * 128:(qb + 1) * 128], op0=MUL, op1=MUL)
                    if e:
                        ins.then_inc(sem["drained7"], 1)
                        dve.wait_ge(sem["drained7"], c.done("drained7"))
                    else:
                        o.link(ins)

            def page(g, b, p):
                if p % 2:
                    dve.wait_ge(sem["full5"], c.done("full5"))
                    dve.wait_ge(sem["qk_done"], c.before("qk_done"))
                    v.tensor_copy(KTs[:, 1, :], bank[5][:, :]).then_inc(sem["drained5"], 1)
                    dve.wait_ge(sem["drained5"], c.done("drained5"))

            def soft_new(g, b):
                dve.wait_ge(sem["qk_done"], c.before("qk_done"))
                dve.wait_ge(sem["bias_sample_in"], c.before("bias_sample_in"))
                v.scalar_tensor_tensor(out=s_all[:, 0:PAGES, :].rearrange("p a b -> p (a b)"), in0=bank[6][:, :], scalar=SCALE,
                                       in1=bP[:], op0=MUL, op1=ADD).then_inc(sem["drained6"], 1)
                dve.wait_ge(sem["drained6"], c.done("drained6"))
                dve.wait_ge(sem["full7"], c.done("full7"))
                v.scalar_tensor_tensor(out=s_all[0:SMP, PAGES, :], in0=bank[7][0:SMP, 0:32], scalar=SCALE,
                                       in1=bN[:, b, :], op0=MUL, op1=ADD).then_inc(sem["drained7"], 1)
                dve.wait_ge(sem["drained7"], c.done("drained7"))
                v.tensor_reduce(mx[:], s_all[:].rearrange("p g j -> p j g"), AX.X, MAX).then_inc(sem["pagemax_ready"], 1)
                dve.wait_ge(sem["pagemax_ready"], c.done("pagemax_ready"))

            def soft_max(g, b):
                dve.wait_ge(sem["full7"], c.done("full7"))
                v.reduce_max(m32[:], bank[7][0:32, 0:128], AX.X).then_inc(sem["drained7"], 1)
                dve.wait_ge(sem["drained7"], c.done("drained7"))
                v.tensor_scalar(dg[:], ident[0:32, 0:32], m32[:], None, MUL).then_inc(sem["diag_ready"], 1)
                dve.wait_ge(sem["diag_ready"], c.done("diag_ready"))

            def soft_exp(g, b):
                dve.wait_ge(sem["full7"], c.done("full7"))
                dve.wait_ge(sem["full6"], c.before("full6"))
                v.tensor_tensor(e_all[:], s_all[:],
                                bank[7][:, 0:32].rearrange("p (o j) -> p o j", o=1).broadcast_to([128, PAGES + 1, 32]), SUB).then_inc(sem["drained7"], 1)
                dve.wait_ge(sem["drained7"], c.done("drained7"))
                dve.wait_ge(sem["e_ready"], c.done("e_ready"))
                v.tensor_reduce(lp[:], e_all[:].rearrange("p g j -> p j g"), AX.X, ADD).then_inc(sem["lsum_ready"], 1)
                dve.wait_ge(sem["lsum_ready"], c.done("lsum_ready"))

            def soft_len(g, b):
                dve.wait_ge(sem["full7"], c.done("full7"))
                v.reciprocal(rl[:], bank[7][:, 0:32]).then_inc(sem["drained7"], 1)
                dve.wait_ge(sem["drained7"], c.done("drained7"))
                one = rl[:].rearrange("p (h c q) -> p h c q", h=2, c=2)[:, :, 1, :]
                o.link(v.tensor_scalar(one, one, lam_neg[:], None, MUL))

            def combine(g, b):
                dve.wait_ge(sem["full6"], c.before("full6"))
                v.tensor_tensor(t64[:].rearrange("p (h e j) -> p h e j", h=2, e=2),
                                bank[6][:, 0:64].rearrange("p (h e j) -> p h e j", h=2, e=2),
                                rl[:].rearrange("p (h o j) -> p h o j", h=2, o=1).broadcast_to([128, 2, 2, 16]), MUL).then_inc(sem["drained6"], 1)
                dve.wait_ge(sem["drained6"], c.done("drained6"))
                t4 = t64[:].rearrange("p (k c q) -> p k c q", k=4, c=2)
                o.link(v.tensor_tensor(oS[:, :, b * NQ:(b + 1) * NQ], t4[:, :, 0, :], t4[:, :, 1, :], ADD))

            def sample_end(g):
                dve.wait_ge(sem["gs_out"], c.before("gs_out"))
                v.tensor_tensor(oQ[:], oS[:], oS[:], MUL).then_inc(sem["sq_ready"], 1)
                dve.wait_ge(sem["sq_ready"], c.done("sq_ready"))
                dve.wait_ge(sem["full7"], c.done("full7"))
                o.link(v.tensor_reduce(rsS[:].rearrange("p (h q) -> p h q", h=2),
                                       bank[7][:, 0:256].rearrange("p (h e q) -> p h q e", h=2, e=2), AX.X, ADD))
                variance(rsS[:], 256).then_inc(sem["drained7"], 1)
                dve.wait_ge(sem["drained7"], c.done("drained7"))
                dve.wait_ge(sem["s_rstd"], c.done("s_rstd"))
                o4 = oS[:].rearrange("p (h e) q -> p h e q", h=2)
                o.link(v.tensor_tensor(o4, o4, rsS[:].rearrange("p (h o q) -> p h o q", h=2, o=1).broadcast_to([128, 2, 2, SMP]), MUL))
                for e in range(2):
                    view = lambda a: a[:].rearrange("p (h e) q -> p h e q", h=2)[:, :, e, :]
                    ins = v.scalar_tensor_tensor(out=view(oQ), in0=view(oS), scalar=subln[:, e:e + 1], in1=view(sgS), op0=MUL, op1=MUL)
                    if e:
                        ins.then_inc(sem["gs_ready"], 1)
                        dve.wait_ge(sem["gs_ready"], c.done("gs_ready"))
                    else:
                        o.link(ins)

            def carry(g):
                for n in ("proj0_drained", "proj1_drained", "drained7", "full6", "full7", "qk_done"):
                    dve.wait_ge(sem[n], c.before(n))
                for hh in range(2):
                    o.link(v.tensor_copy(qS[:, 2 * hh:2 * hh + 2, :], qT[hh][:, :, SEQ:T]))
                    o.link(v.tensor_copy(kS[:, 2 * hh:2 * hh + 2, :], kT[hh][:, :, SEQ:T]))
                    o.link(v.tensor_copy(vS[0:SMP, hh * 256:hh * 256 + 256], vn[hh][0:SMP, 4, :]))
                v.tensor_copy(sgS[:], sgN[:]).then_inc(sem["carried"], 1)
                dve.wait_ge(sem["carried"], c.done("carried"))

            def rope_(g, which):
                for n in ("proj0_drained", "proj1_drained"):
                    dve.wait_ge(sem[n], c.before(n))
                dve.wait_ge(rope_in, 16)
                for n in ("full4", "full5"):
                    dve.wait_ge(sem[n], c.before(n))
                dst = (rqT, rkT)[which]
                cos, sin = rope[:, 0:T], rope[:, T:2 * T]
                o.link(v.tensor_tensor(dst[:, 0, :], raw[:, 0, :], cos, MUL))
                o.link(v.tensor_tensor(rt[:, 0, :], raw[:, 1, :], sin, MUL))
                o.link(v.tensor_tensor(dst[:, 0, :], dst[:, 0, :], rt[:, 0, :], SUB))
                o.link(v.tensor_tensor(dst[:, 1, :], raw[:, 0, :], sin, MUL))
                o.link(v.tensor_tensor(rt[:, 1, :], raw[:, 1, :], cos, MUL))
                v.tensor_tensor(dst[:, 1, :], dst[:, 1, :], rt[:, 1, :], ADD).then_inc(sem["rotated"], 1)
                dve.wait_ge(sem["rotated"], c.done("rotated"))

            def ret_scores(g, c_):
                lo = c_ * 128
                dve.wait_ge(sem["head_in"], c.before("head_in"))
                dve.wait_ge(sem["full6"], c.before("full6"))
                dve.wait_ge(sem["full4"], c.done("full4"))
                v.tensor_tensor(sT[:], bank[4][:, 0:128], hc[:, 0:128], MUL).then_inc(sem["drained4"], 1)
                dve.wait_ge(sem["drained4"], c.done("drained4"))
                for e in range(2):
                    ins = v.tensor_tensor(qd[:, e, :], rqT[:, e, lo:lo + 128], hc[:, 128:256], MUL)
                    if e:
                        ins.then_inc(sem["qd_ready"], 1)
                        dve.wait_ge(sem["qd_ready"], c.done("qd_ready"))
                    else:
                        o.link(ins)

            def ret_state(g, c_):
                dve.wait_ge(sem["full6"], c.before("full6"))
                dve.wait_ge(sem["sp_out"], c.before("sp_out"))
                for e in range(2):
                    dve.wait_ge(sem[f"full{4 + e}"], c.done(f"full{4 + e}"))
                    if c_:
                        ins = v.scalar_tensor_tensor(out=Sp[:, e, :], in0=Sp[:, e, :], scalar=hc[:, 393:394], in1=bank[4 + e][:, :],
                                                     op0=MUL, op1=ADD)
                    else:
                        ins = v.tensor_copy(Sp[:, e, :], bank[4 + e][:, :])
                    ins.then_inc(sem[f"drained{4 + e}"], 1)
                    dve.wait_ge(sem[f"drained{4 + e}"], c.done(f"drained{4 + e}"))

            def ret_norm(g, t):
                R = TILES[t][1]
                dve.wait_ge(sem["drained6"], c.before("drained6"))
                o.link(v.tensor_tensor_reduce(out=rjunk[0:R, :], in0=oN[0:R, t, :], in1=oN[0:R, t, :], scale=1.0, scalar=0.0,
                                              op0=MUL, op1=ADD, accum_out=rst[0:R, 0:1]))
                variance(rst[0:R, 0:1], 512).then_inc(sem["o_var"], 1)
                dve.wait_ge(sem["o_var"], c.done("o_var"))
                dve.wait_ge(sem["o_rstd"], c.done("o_rstd"))
                v.tensor_scalar(oN[0:R, t, :], oN[0:R, t, :], rst[0:R, 1:2], None, MUL).then_inc(sem["o_normed"], 1)
                dve.wait_ge(sem["o_normed"], c.done("o_normed"))

            def rs_scores(g):
                dve.wait_ge(sem["full6"], c.before("full6"))
                dve.wait_ge(sem["full4"], c.done("full4"))
                v.tensor_tensor(sT[0:SMP, 0:SMP], bank[4][0:SMP, 0:SMP], hc[0:SMP, 320:384], MUL).then_inc(sem["drained4"], 1)
                dve.wait_ge(sem["drained4"], c.done("drained4"))
                o.link(v.memset(qz[:], 0.0))
                for e in range(2):
                    o.link(v.tensor_tensor(qz[:, e, :].rearrange("p (b r) -> p b r", r=72)[:, :, 0:8],
                                           rqT[:, e, SEQ:T].rearrange("p (b i) -> p b i", i=8),
                                           hc[:, 256:320].rearrange("p (b i) -> p b i", i=8), MUL))
                dve.wait_ge(sem["full5"], c.done("full5"))
                for b in range(NB):
                    ins = v.tensor_scalar(kz[:, b, :], bank[5][0:SMP, 0:256], hc[0:SMP, 384 + b:385 + b], None, MUL)
                    if b == NB - 1:
                        ins.then_inc(sem["qd_ready"], 1)
                        dve.wait_ge(sem["qd_ready"], c.done("qd_ready"))
                    else:
                        o.link(ins)
                dve.nop().then_inc(sem["drained5"], 1)

            def rs_state(g, b):
                dve.wait_ge(sem[f"state_out{b % 2}"], c.before(f"state_out{b % 2}"))
                for e in range(2):
                    dve.wait_ge(sem[f"full{4 + e}"], c.done(f"full{4 + e}"))
                    cols = slice(e * 512, (e + 1) * 512)
                    v.scalar_tensor_tensor(out=Sout[:, b % 2, cols], in0=Sin[:, b % 3, cols], scalar=hc[:, 394:395],
                                           in1=bank[4 + e][:, :], op0=MUL, op1=ADD).then_inc(sem[f"drained{4 + e}"], 1)
                    dve.wait_ge(sem[f"drained{4 + e}"], c.done(f"drained{4 + e}"))

            def gate(g, t):
                n, R = 4 + t % 2, TILES[t][1]
                for m in ("proj0_drained", "proj1_drained", f"gt_out{t % 2}"):
                    dve.wait_ge(sem[m], c.before(m))
                dve.wait_ge(sem[f"full{n}"], c.done(f"full{n}"))
                v.tensor_tensor(gt[:, t % 2, :].rearrange("p (k t) -> p k t", k=4)[:, :, 0:R],
                                bank[n][:, :].rearrange("p (k t) -> p k t", k=4)[:, :, 0:R],
                                rsg[:, :, t * 128:t * 128 + R], MUL).then_inc(sem[f"drained{n}"], 1)
                dve.wait_ge(sem[f"drained{n}"], c.done(f"drained{n}"))

            def norm_tile(g, t, stage):
                R = TILES[t][1]
                if stage:
                    dve.wait_ge(sem["y_drained"], c.done("y_drained"))
                    o.link(v.tensor_tensor_reduce(out=njunk[0:R, :], in0=yn[0:R, :], in1=yn[0:R, :], scale=1.0, scalar=0.0,
                                                  op0=MUL, op1=ADD, accum_out=nst[0:R, 0:1]))
                    variance(nst[0:R, 0:1], D).then_inc(sem["y_var"], 1)
                    dve.wait_ge(sem["y_var"], c.done("y_var"))
                    dve.wait_ge(wpost_in, 16 * stage)
                    dve.wait_ge(sem["y_rstd"], c.done("y_rstd"))
                    o.link(v.scalar_tensor_tensor(out=yn[0:R, :], in0=yn[0:R, :], scalar=nst[0:R, 1:2], in1=wpost[0:R, :],
                                                  op0=MUL, op1=MUL))
                dve.wait_ge(sem["x_in"], c.done("x_in"))
                if stage:
                    v.tensor_tensor(xt[0:R, :], xt[0:R, :], yn[0:R, :], ADD).then_inc(sem["x_sum"], 1)
                    dve.wait_ge(sem["x_sum"], c.done("x_sum"))
                if stage < 2:
                    o.link(v.tensor_tensor_reduce(out=njunk[0:R, :], in0=xt[0:R, :], in1=xt[0:R, :], scale=1.0, scalar=0.0,
                                                  op0=MUL, op1=ADD, accum_out=nst[0:R, 2:3]))
                    variance(nst[0:R, 2:3], D).then_inc(sem["x_var"], 1)
                    dve.wait_ge(sem["x_var"], c.done("x_var"))
                    dve.wait_ge(sem["x_hi"], c.done("x_hi"))
                    for j in range(KT):
                        xc = slice(t * 128, t * 128 + R)
                        ins = v.scalar_tensor_tensor(out=XL[:, j, xc], in0=bank[j // 4][:, (j % 4) * 128:(j % 4) * 128 + R],
                                                     scalar=wpre[:, stage, j:j + 1], in1=XH[:, j, xc].bitcast(f32), op0=MUL, op1=SUB)
                        if j == KT - 1:
                            ins.then_inc(sem["x_lo"], 1)
                            dve.wait_ge(sem["x_lo"], c.done("x_lo"))
                        else:
                            o.link(ins)

            run(dve, c, o, dict(mask_rows=mask_rows, relay_area=all_done(dve, c), split_w=split_w, split_g=split_g, evacuate=evacuate, scores=scores, pv=pv, o_transpose=o_transpose,
                                page=page, soft_new=soft_new, soft_max=soft_max, soft_exp=soft_exp, soft_len=soft_len,
                                combine=combine, sample_end=sample_end, carry=carry, rope=rope_,
                                ret_scores=lambda g, c: ret_scores(g, c), ret_state=lambda g, c: ret_state(g, c),
                                ret_norm=ret_norm, rs_scores=rs_scores, rs_state=rs_state, gate=gate, norm_tile=norm_tile))

        @block.gpsimd
        def _(pool):
            c = Count()

            begin(pool, POOL_NAMES)
            pool.nop().then_inc(starts_done, 1)
            pool.wait_ge(starts_done, 5)
            pool.wait_ge(setup_done, 2)
            pool.wait_ge(lam_dot, 1)

            def rsqrt(out, a, name, R=128, n=1):
                nc.gpsimd.tensor_tensor(out, a, power[0:R, 0:n], ALU.pow).then_inc(sem[name], 1)

            def pv(g, hp, qb, back):
                pool.wait_ge(sem["o_var"], c.done("o_var"))
                rsqrt(pst[:, 7:8], pst[:, 6:7], "o_rstd")

            def sample_end(g):
                pool.wait_ge(sem["drained7"], c.done("drained7"))
                rsqrt(rsS[:], rsS[:], "s_rstd", n=128)

            def ret_norm(g, t):
                R = TILES[t][1]
                pool.wait_ge(sem["o_var"], c.done("o_var"))
                rsqrt(rst[0:R, 1:2], rst[0:R, 0:1], "o_rstd", R)

            def norm_tile(g, t, stage):
                R = TILES[t][1]
                if stage:
                    pool.wait_ge(sem["y_var"], c.done("y_var"))
                    rsqrt(nst[0:R, 1:2], nst[0:R, 0:1], "y_rstd", R)
                if stage < 2:
                    pool.wait_ge(sem["x_var"], c.done("x_var"))
                    rsqrt(nst[0:R, 3:4], nst[0:R, 2:3], "x_rstd", R)

            run(pool, c, None, dict(pv=pv, sample_end=sample_end, ret_norm=ret_norm, norm_tile=norm_tile))


_INS = ["x_prompt", "x_sample", "cache_k", "cache_v", "page_table", "state_ret", "norm_pre_attn", "w_in_attn",
        "lambda_q1", "lambda_k1", "lambda_q2", "lambda_k2", "subln_w_attn", "w_out_attn", "norm_post_attn",
        "norm_pre_ret", "w_in_ret", "w_out_ret", "norm_post_ret"]
_OUTS = [(1, SEQ, D), (NB, NQ, D), (1, SEQ, HEADS, 256), (1, SEQ, HEADS, 256), (1, HEADS, 256, 512),
         (NB, NQ, HEADS, 256), (NB, NQ, HEADS, 256), (NB, HEADS, 256, 512)]


def kernel(**inputs):
    import numpy as _np
    import concourse.bacc as _bacc
    from concourse import mybir as _mybir
    from concourse.bass_utils import run_bass_kernel_spmd as _run

    nc = _bacc.Bacc("TRN2", target_bir_lowering=False, num_devices=1)
    arrays, args = {}, []
    for name in _INS:
        a = _np.ascontiguousarray(inputs[name])
        arrays[f"in_{name}"] = a
        args.append(nc.dram_tensor(f"in_{name}", a.shape, _mybir.dt.from_np(a.dtype), kind="ExternalInput").ap())
    for i, shape in enumerate(_OUTS):
        args.append(nc.dram_tensor(f"out_{i}", shape, _mybir.dt.float32, kind="ExternalOutput").ap())
    hybrid_step_kernel(nc, *args)
    r = _run(nc, [arrays], core_ids=[0])
    return tuple(r.results[0][f"out_{i}"] for i in range(len(_OUTS)))
```

```python
import concourse.bass as bass
from concourse import mybir
from contextlib import ExitStack
import math
import numpy as np

D = 2048
SEQ = 512
NB, NQ = 8, 8
SMP = NB * NQ
T = SEQ + SMP
HALF = T // 2
PAST, PAGE = 2048, 128
PAGES = PAST // PAGE
HEADS = 8
EPS = 1e-6
LAMBDA_INIT = 0.8 - 0.6 * math.exp(-0.3 * 0)
SCALE = 128 ** -0.5
KT = D // 128
CH = 4
NCH = KT // CH
TILES = [(t, min(128, T - 128 * t)) for t in range(5)]
MASKED = -1e30
HC = 128 + 128 + 64 + 64 + 8 + 1 + 2
RING = {"k": 4, "v": 8}
GROUP = 4
NPAIR = 1 + PAGES // GROUP + 1


def shape_tables():
    slope = 2.0 ** -np.arange(1, 9)
    q, j = np.arange(128)[:, None], np.arange(512)[None]
    dist = q + 384 - j
    bias_prompt = np.stack([np.where(dist >= 0, -s * dist, MASKED) for s in slope])
    head, half, tok = [a.reshape(-1) for a in np.meshgrid(range(2), range(2), range(NQ), indexing="ij")]
    dist_past = PAST + tok[:, None] - np.arange(GROUP * PAGE)[None]
    pick = (head[:, None] == np.arange(2)[None]).repeat(NQ, 1) * np.tile(tok[:, None] == np.arange(NQ)[None], (1, 2))
    rows = np.concatenate([dist_past, pick * (half == 0)[:, None], pick * (half == 1)[:, None]], 1)
    row = np.arange(SMP)
    pairs = []
    for g in range(HEADS // 2):
        sl = slope[2 * g + head][:, None]
        ahead = sl * GROUP * PAGE * np.arange(PAGES // GROUP)[None]
        dn = tok[:, None, None] - (row % NQ)[None, None]
        own = (row // NQ)[None, None] == np.arange(NB)[None, :, None]
        new = np.where(own & (dn >= 0), -sl[:, :, None] * dn, MASKED)
        pairs.append(np.concatenate([-sl, ahead, 0 * sl, new.reshape(32, NB * SMP)], 1))
    bias_pairs = np.stack(pairs)
    f = np.float32
    inv = (f(1.0) / (f(10000.0) ** np.linspace(0.0, 1.0, 128, dtype=f))).astype(f)
    where = np.concatenate([np.arange(SEQ), PAST + np.tile(np.arange(NQ), NB)]).astype(f)
    ang = (inv[:, None] * where[None]).astype(f).astype(np.float64)
    rope = np.concatenate([np.cos(ang), np.sin(ang)], 1)
    heads = []
    i = np.arange(128.0)
    for h in range(HEADS):
        lg = math.log1p(-2.0 ** (-5 - h))
        w = 1.0 / 16
        diff = i[None] - i[:, None]
        dec = np.where(diff >= 0, np.exp(lg * np.maximum(diff, 0)), 0) * w
        t = row % NQ
        ds = t[None] - t[:, None]
        decs = np.where((ds >= 0) & (row[None] // NQ == row[:, None] // NQ), np.exp(lg * np.maximum(ds, 0)), 0) * w
        pad = lambda a: np.concatenate([a, np.zeros((128 - a.shape[0], a.shape[1]))])
        spread = lambda a: np.broadcast_to(a[None], (128, a.size))
        kz = np.where(row[:, None] // NQ == np.arange(NB)[None], np.exp(lg * (NQ - 1.0 - t))[:, None], 0) * w
        heads.append(np.concatenate([dec, spread(np.exp(lg * (i + 1))), spread(np.exp(lg * (t + 1.0))), pad(decs), pad(kz),
                                     (np.exp(lg * (127.0 - i)) * w)[:, None],
                                     spread(np.exp(lg * np.array([128.0, 8.0])))], 1))
    eye = np.concatenate([np.eye(128), np.ones((128, 128))], 1)
    return [np.ascontiguousarray(a, dtype=f) for a in (bias_prompt, rows, bias_pairs, rope, np.stack(heads), eye)]


class Stage:
    def __init__(self, kind, /, **a):
        self.kind, self.a, self.upto = kind, a, {}


def adds(s):
    k, a = s.kind, s.a
    if k in ("relay_area", "load_rope", "row_tables"):
        return {}
    if k == "load_w":
        return {f"w_in{a['slot']}": 16}
    if k == "load_g":
        return {f"gated_in{a['kt'] // CH}": 16}
    if k == "split_w" or k == "split_g":
        return {"w_hi": 1, "w_lo": 1}
    if k == "project":
        i = a["i"]
        return {**({"w_used": 1} if i % 8 == 7 else {}), **({"proj0_full": 1} if i == 27 else {})}
    if k == "evacuate":
        return {f"proj{a['cb']}_drained": 1}
    if k == "rope":
        return {"rotated": 1}
    if k == "y_tile":
        return {f"x_in{a['t'] % 2}": 16, "y_full": 1, "y_sq": 1, "y_var": 1, "y_rstd": 1, "y_used": 1, "x_sum": 1}
    if k == "x_tile":
        return {**({} if a["stage"] else {f"x_in{a['t'] % 2}": 16}),
                "x_sq": 1, "x_var": 1, "x_rstd": 1, "x_normed": 1, "xt_full": 1, "x_hi": 4, "x_lo": 1}
    if k == "store_x":
        return {f"x_out{a['t'] % 2}": 16}
    table = {
        "load_bias_prompt": {"bias_prompt_in": 16}, "load_bias_sample": {"bias_sample_in": 16},
        "load_head": {"head_in": 16},
        "scores": {"full4": 1, "full5": 1, "drained4": 1, "drained5": 1, "max_ready": 1, "exp_ready": 1, "p_ready": 1},
        "p_transpose": {"full7": 1, "drained7": 1},
        "pv": {"full7": 1, "drained7": 1, "o_var": 1, "o_rstd": 1, "o_normed": 1},
        "o_transpose": {"full7": 1, "drained7": 1},
        "store_gated": {"gated_out": 16},
        "natural": {"full7": 1, "drained7": 1},
        "store_natural": {"natural_out": 32},
        "qk": {"full6": 1, "drained6": 1},
        "place_q": {"q_placed": 1},
        "soft_new": {"full7": 1, "drained7": 1, "rows_ready": 1},
        "soft_exp": {"e_rows": 1, "mix_ready": 1},
        "e_transpose": {"full4": 1, "full5": 1, "drained4": 1, "drained5": 1},
        "value": {"pv_done": 1}, "value_new": {"full6": 1, "drained6": 1},
        "mix": {"full7": 1, "drained7": 1},
        "sample_end": {"sq_ready": 1, "full7": 1, "drained7": 1, "s_rstd": 1, "gs_ready": 1},
        "store_sample": {"gs_out": 16},
        "carry": {"carried": 1},
        "ret_scores": {"full4": 1, "full5": 1, "drained4": 1, "drained5": 1, "qd_ready": 1},
        "ret_out": {"full6": 1, "drained6": 1},
        "ret_state": {"full4": 1, "full5": 1, "drained4": 1, "drained5": 1},
        "store_state_p": {"sp_out": 16},
        "rs_scores": {"full4": 1, "full5": 1, "drained4": 1, "drained5": 1, "qd_ready": 1},
        "rs_intra": {}, "rs_out": {"full6": 1, "drained6": 1},
        "rs_state": {"full4": 1, "full5": 1, "drained4": 1, "drained5": 1},
        "ret_norm": {"o_var": 1, "o_rstd": 1, "o_normed": 1},
    }
    if k in table:
        return table[k]
    if k in ("load_k", "load_v"):
        return {f"{k[-1]}_in{a['p'] % RING[k[-1]]}": 16}
    if k == "load_state":
        return {f"state_in{a['b'] % 3}": 16}
    if k == "store_state":
        return {f"state_out{a['b'] % 2}": 16}
    if k == "page":
        n = 4 + a["p"] % 2
        return {f"full{n}": 1, f"drained{n}": 1}
    if k == "gate":
        n = 4 + a["t"] % 2
        return {f"full{n}": 1, f"drained{n}": 1}
    if k == "store_ret":
        return {"gt_out%d" % (a["t"] % 2): 16}
    raise KeyError(k)


class Segment:
    def __init__(self, stages, times=1, first=0):
        self.stages, self.times, self.first = stages, times, first


def first_weights(chunk, between=()):
    return ([Stage("load_w", slot=m, **chunk(m)) for m in (0, 1)] + list(between)
            + [Stage("split_w", slot=0), Stage("load_w", slot=0, **chunk(2))])


def project_step(out, i0, w, cols, coef, kinds, inserts, n0, last, krow=0):
    for i in range(32):
        n = n0 * NCH + i // 8
        for s in inserts.get(i, []):
            out.append(s)
        out.append(Stage("project", i=i))
        if i % 8 == 2 and not (last and i // 8 == NCH - 1):
            out.append(Stage("split_w", slot=(n + 1) % 2))
            if i0(n + 3) is not None:
                out.append(Stage("load_w", slot=(n + 1) % 2, **i0(n + 3)))
        if i == 28:
            out.append(Stage("evacuate", cb=0, **kinds))
    for s in inserts.get(32, []):
        out.append(s)
    out.append(Stage("evacuate", cb=1, **kinds))


def prompt_stages(hp, qb):
    return {0: [Stage("scores", hp=hp, qb=qb)], 12: [Stage("p_transpose", hp=hp, qb=qb)], 14: [Stage("pv", hp=hp, qb=qb)],
            28: [Stage("o_transpose", hp=hp, qb=qb)], 30: [Stage("store_gated", hp=hp, qb=qb)]}


def sample_stages(b):
    at = {}

    def put(i, *s):
        at.setdefault(i, []).extend(s)

    def ahead(kind, p):
        p += RING[kind[-1]]
        if p < PAGES:
            return [Stage(kind, b=b, p=p)]
        return [Stage(kind, b=b + 1, p=p - PAGES)] if b + 1 < NB else []
    put(0, Stage("place_q", b=b))
    if b == 0:
        for p in range(RING["v"]):
            put(4 + p, Stage("load_v", b=0, p=p))
    if b:
        put(1, Stage("mix", b=b - 1))
    for p in range(PAGES):
        if p and p % GROUP == 0:
            put(2 + p, Stage("qk", b=b, group=p // GROUP - 1))
        put(2 + p, Stage("page", b=b, p=p), *ahead("load_k", p))
    put(18, Stage("qk", b=b, group=PAGES // GROUP - 1), Stage("soft_new", b=b), Stage("soft_exp", b=b))
    put(24, Stage("e_transpose", b=b))
    for p in range(PAGES):
        put(25 + p * 7 // PAGES, Stage("value", b=b, p=p), *ahead("load_v", p))
    put(32, Stage("value_new", b=b))
    if b == NB - 1:
        put(32, Stage("mix", b=b))
    return at


def merge(*ds):
    out = {}
    for d in ds:
        for i, s in d.items():
            out.setdefault(i, []).extend(s)
    return out


def attention_pair(first, project, last=False):
    def chunk(n):
        if n >= 8 * NCH:
            return None
        s, c = divmod(n, NCH)
        return dict(w="in0", row=c * CH, cols=(s % 4) * D + (s // 4) * 256, coef=512)
    keys = [] if first else [Stage("load_k", b=0, p=p) for p in range(RING["k"])]
    out = first_weights(chunk, keys) if project else keys
    if first:
        out += [Stage("relay_area"), Stage("row_tables")]
    else:
        out.append(Stage("load_bias_sample"))
    for s in range(8):
        hh, kind = divmod(s, 4)
        ins = {}
        if not (first and s < 4) and not (last and s >= 4):
            hp = (hh + 1) % 2
            if kind == 0:
                out.append(Stage("load_bias_prompt", head=hh - 1))
            ins = prompt_stages(hp, kind)
            for i in ins:
                for x in ins[i]:
                    x.a["back"] = hh - 1
        if not first:
            ins = merge(ins, sample_stages(s))
        if project and kind >= 2:
            what = "kv"[kind - 2]
            ins = merge(ins, {3 + 3 * j: [Stage("natural", what=what, hh=hh, j=j)] for j in range(3)},
                        {13: [Stage("store_natural", what=what, hh=hh)]})
        if project:
            project_step(out, chunk, "in0", 0, 0, dict(kind="qkvg"[kind], hh=hh), ins, s, s == 7)
        else:
            for i in range(33):
                out += ins.get(i, [])
    if not first:
        out += [Stage("sample_end"), Stage("store_sample")]
    if project:
        out.append(Stage("carry"))
    return out


def outer_projection(w, krow, add):
    def chunk(n):
        if n >= 8 * NCH:
            return None
        s, c = divmod(n, NCH)
        return dict(w=w, row=krow + c * CH, cols=s * 256, coef=0)
    out = first_weights(chunk) + ([] if add else [Stage("relay_area")])
    for k in range(0, KT, CH):
        out.append(Stage("load_g", layer=w, row=krow + k, kt=k))
    for s in range(8):
        project_step(out, chunk, w, 0, 0, dict(kind="+" if add else "y", hh=s), 
                     {8 * n: [Stage("split_g", kt=n * CH + k) for k in range(CH)] for n in range(NCH)} if s == 0 else {}, s, s == 7)
    return out


def retention_head():
    cols = [(0, 256), (D, 256), (2 * D, 512), (2 * D + 256, 512), (4 * D, 512), (4 * D + 256, 512)]
    cols[4], cols[5] = (2 * D + 2 * D, 512), (2 * D + 2 * D + 256, 512)

    def chunk(n):
        if n >= 6 * NCH:
            return None
        s, c = divmod(n, NCH)
        return dict(w="in1", row=c * CH, cols=cols[s][0], coef=cols[s][1])
    out = first_weights(chunk)
    for s in range(6):
        ins = {8: [Stage("load_head")] + [Stage("load_state", b=b) for b in range(3)]} if s == 0 else {}
        if s in (3, 4):
            ins = merge(ins, {2 + 2 * j: [Stage("natural", what="r", hh=s - 3, j=j)] for j in range(3)})
        if s == 4:
            for c in range(4):
                ins = merge(ins, {8 + 6 * c: [Stage("ret_scores", c=c)], 11 + 6 * c: [Stage("ret_out", c=c)],
                                  12 + 6 * c: [Stage("ret_state", c=c)], 13 + 6 * c: [Stage("ret_norm", t=c)]})
        if s == 5:
            ins = merge(ins, {0: [Stage("store_state_p"), Stage("rs_scores")], 7: [Stage("rs_intra")]})
            for b in range(NB):
                ins = merge(ins, {8 + 5 * b // 2: [Stage("rs_state", b=b)],
                                  10 + 5 * b // 2: [Stage("store_state", b=b)] + ([Stage("load_state", b=b + 3)] if b + 3 < NB else [])})
            ins = merge(ins, {28: [Stage("rs_out")], 29: [Stage("ret_norm", t=4)]})
        project_step(out, chunk, "in1", 0, 0, dict(kind=["q", "k", "v", "v", "g", "g"][s] + "r", hh=s % 2), ins, s, s == 5)
        if s < 2:
            out.append(Stage("rope", which=s))
    for t in range(5):
        out.append(Stage("gate", t=t))
        out.append(Stage("store_ret", t=t))
    return out


def norm_segment(stage):
    out = []
    for t in range(6):
        if stage and t < 5:
            out.append(Stage("y_tile", t=t, stage=stage))
        if stage and t:
            out.append(Stage("store_x", t=t - 1, stage=stage))
        if stage < 2 and t:
            out.append(Stage("x_tile", t=t - 1, stage=stage))
    return out


def plan():
    segs = [Segment(norm_segment(0)),
            Segment(attention_pair(True, True)),
            Segment(attention_pair(False, True), times=3, first=1),
            Segment(attention_pair(False, False, last=True), first=4),
            Segment(outer_projection("out0", 0, False)),
            Segment(norm_segment(1)),
            Segment([Stage("relay_area"), Stage("load_rope")]),
            Segment(retention_head(), times=8),
            Segment(outer_projection("out1", 0, False)),
            Segment(outer_projection("out1", KT, True)),
            Segment(norm_segment(2))]
    names = {}
    for seg in segs:
        total = {}
        for s in seg.stages:
            for name, n in adds(s).items():
                total[name] = total.get(name, 0) + n
                names[name] = n
            s.upto = dict(total)
        seg.total = total
    return segs, sorted(names)


def hybrid_step_kernel(nc, x_prompt, x_sample, cache_k, cache_v, page_table, state_ret, norm_pre_attn, w_in_attn,
                       lambda_q1, lambda_k1, lambda_q2, lambda_k2, subln_w_attn, w_out_attn, norm_post_attn,
                       norm_pre_ret, w_in_ret, w_out_ret, norm_post_ret,
                       y_prompt, y_sample, k_prompt, v_prompt, ret_state_prompt, k_sample, v_sample, ret_state_sample):
    f32, f32r, i32 = mybir.dt.float32, mybir.dt.float32r, mybir.dt.int32
    ALU, ACT, AX = mybir.AluOpType, mybir.ActivationFunctionType, mybir.AxisListType
    MUL, ADD, SUB, MAX = ALU.mult, ALU.add, ALU.subtract, ALU.max

    segs, sem_names = plan()
    bias_prompt_d, rows_d, bias_pairs_d, rope_d, heads_d, eye_d = [
        nc.inline_tensor(a, name=n)[tuple(slice(None) for _ in a.shape)] for a, n in
        zip(shape_tables(), ("bias_prompt", "score_rows", "bias_pairs", "rope", "ret_heads", "eye"))]
    gated0_d = nc.dram_tensor("gated_attention", (D, T), f32, kind="Internal").ap()
    gated1_d = nc.dram_tensor("gated_retention", (2 * D, T), f32, kind="Internal").ap()
    x1_d = nc.dram_tensor("x_between_layers", (T, D), f32, kind="Internal").ap()

    weights = {"in0": w_in_attn, "in1": w_in_ret, "out0": w_out_attn, "out1": w_out_ret}
    weights = {k: v.rearrange("(k p) n -> p k n", p=128) for k, v in weights.items()}
    gated = {"out0": gated0_d.rearrange("(k p) t -> p k t", p=128), "out1": gated1_d.rearrange("(k p) t -> p k t", p=128)}
    ck = cache_k.rearrange("n s h d -> n s (h d)")
    cv = cache_v.rearrange("n s h d -> n s (h d)")
    xp, xs = x_prompt.rearrange("b s d -> (b s) d"), x_sample.rearrange("b s d -> (b s) d")
    yp, ys = y_prompt.rearrange("b s d -> (b s) d"), y_sample.rearrange("b s d -> (b s) d")
    natural_out = {"k": (k_prompt, k_sample), "v": (v_prompt, v_sample)}
    natural_out = {k: (a.rearrange("b (t p) h d -> p (b t) (h d)", p=128), b.rearrange("b s h d -> (b s) (h d)"))
                   for k, (a, b) in natural_out.items()}
    st_in = state_ret.rearrange("b h (e p) v -> (b h) p e v", p=128)
    st_out = ret_state_sample.rearrange("b h (e p) v -> (b h) p e v", p=128)
    sp_out = ret_state_prompt.rearrange("b h (e p) v -> (b h) p e v", p=128)

    ctx = ExitStack()
    with ctx:
        def sb(name, shape, dt=f32):
            return ctx.enter_context(nc.sbuf_tensor(name, shape, dt))

        XH, XL = sb("XH", [128, KT, T], f32r), sb("XL", [128, KT, T], f32r)
        WR = sb("WR", [128, 2, CH, 256])
        WH, WL = sb("WH", [128, 2, CH, 256], f32r), sb("WL", [128, 2, CH, 256], f32r)
        eye = sb("eye_sb", [128, 256])
        pt = sb("pt", [1, NB * PAGES], i32)
        wpre = sb("wpre", [128, 2, KT])
        subln = sb("subln", [128, 2])
        lam_neg = sb("lam_neg", [128, 1])
        power = sb("power", [128, 128])
        small = sb("small", [128, 8])
        ident, ones = eye[:, 0:128], eye[:, 128:256]
        AREA = 27900
        area = sb("area", [128, AREA])
        used = [0]

        def lay(name, shape, dt=f32):
            n = int(np.prod(shape[1:]))
            lo = used[0]
            used[0] += n
            assert used[0] <= AREA, (name, used[0])
            a = area[0:shape[0], lo:lo + n]
            if dt is not f32:
                a = a.bitcast(dt)
            if len(shape) == 3:
                a = a.rearrange("p (a b) -> p a b", a=shape[1])
            if len(shape) == 4:
                a = a.rearrange("p (a b c) -> p a b c", a=shape[1], b=shape[2])
            return a

        qT, kT = [lay(f"qT{i}", [128, 2, T]) for i in range(2)], [lay(f"kT{i}", [128, 2, T]) for i in range(2)]
        vT, sg = lay("vT", [128, 2, T]), lay("sg", [128, 2, T])
        vn, kn = [lay(f"vn{i}", [128, 5, 256]) for i in range(2)], lay("kn", [128, 5, 256])
        qS, kS, sgN, sgS = [lay(n, [128, 4, SMP]) for n in ("qS", "kS", "sgN", "sgS")]
        vS = lay("vS", [128, 512])
        sS, sN = lay("sS", [32, PAST]), lay("sN", [32, SMP])
        e_all, e_new = lay("e_all", [128, PAGES, 32]), lay("e_new", [SMP, 32])
        dist_past, picks = lay("dist_past", [32, GROUP * PAGE]), lay("picks", [32, 32])
        pair_row = lay("pair_row", [32, NPAIR + NB * SMP])
        KTs = lay("KTs", [128, 4, GROUP * PAGE])
        qrow = lay("qrow", [128, 160])
        pick_lam, mixw = lay("pick_lam", [32, 16]), lay("mixw", [32, 16])
        gmax, ebias, lsum, row1 = lay("gmax", [32, 5]), lay("ebias", [32, 5]), lay("lsum", [32, 5]), lay("row1", [32, 2])
        oS, oQ = lay("oS", [128, 4, SMP]), lay("oQ", [128, 4, SMP])
        rsS = lay("rsS", [128, 128])
        sc, pT = lay("sc", [128, 2, 512]), lay("pT", [128, 512])
        oP, gP, bH = lay("oP", [128, 256]), lay("gP", [128, 2, 128]), lay("bH", [128, 512])
        junk = lay("junk", [128, 256])
        pst = lay("pst", [128, 8])
        Kr, Vr = lay("Kr", [128, RING["k"], 512]), lay("Vr", [128, RING["v"], 512])
        used[0] = 0
        rope, hc = lay("rope_sb", [128, 2 * T]), lay("hc", [128, HC])
        raw, rqT, rkT = lay("raw", [128, 2, T]), lay("rqT", [128, 2, T]), lay("rkT", [128, 2, T])
        rt = lay("rt", [128, 2, T])
        rvT, rvn, rsg, oN = lay("rvT", [128, 2, T]), lay("rvn", [128, 5, 512]), lay("rsg", [128, 4, T]), lay("oN", [128, 5, 512])
        Sp, Sin, Sout = lay("Sp", [128, 2, 512]), lay("Sin", [128, 3, 1024]), lay("Sout", [128, 2, 1024])
        qd, kd, sT = lay("qd", [128, 2, 128]), lay("kd", [128, 256]), lay("sT", [128, 128])
        qz, kz, gt = lay("qz", [128, 2, T]), lay("kz", [SMP, NB, 256]), lay("gt", [128, 2, 4 * 128])
        rjunk, rst = lay("rjunk", [128, 512]), lay("rst", [128, 4])
        used[0] = 0
        yT = lay("yT", [128, KT, T])
        gstage = lay("gstage", [128, KT, T])
        used[0] = KT * T
        xt, yn, njunk, wpost = lay("xt", [128, 2, D]), lay("yn", [128, 2, D]), lay("njunk", [128, D]), lay("wpost", [128, D])
        nst = lay("nst", [128, 2, 4])

        low, high = [ctx.enter_context(nc.psum_tensor(n, [128, 4, 512], f32)) for n in ("low_banks", "high_banks")]
        bank = [(low, high)[i // 4][:, i % 4, :] for i in range(8)]

        sem = {n: ctx.enter_context(nc.semaphore(n)) for n in sem_names}
        const_in = ctx.enter_context(nc.semaphore("const_in"))
        page_table_in = ctx.enter_context(nc.semaphore("page_table_in"))
        wpost_in, wpost_free = ctx.enter_context(nc.semaphore("wpost_in")), ctx.enter_context(nc.semaphore("wpost_free"))
        rows_in = ctx.enter_context(nc.semaphore("rows_in"))
        rope_in = ctx.enter_context(nc.semaphore("rope_in"))
        setup_done = ctx.enter_context(nc.semaphore("setup_done"))
        lam_exp = ctx.enter_context(nc.semaphore("lam_exp"))
        lam_dot = ctx.enter_context(nc.semaphore("lam_dot"))
        starts_done = ctx.enter_context(nc.semaphore("starts_done"))
        sp_passed = ctx.enter_context(nc.semaphore("sp_passed"))
        pe_passed = ctx.enter_context(nc.semaphore("pe_passed"))
        chain_sem = {e: ctx.enter_context(nc.semaphore(f"{e}_order")) for e in ("dve", "act", "pool")}

        def start_of(name):
            return 16 if name.endswith("_out") or "_out" in name else 1

        DMA_NAMES = {n for n in sem_names if "_in" in n or "_out" in n}
        START = {n: (16 if n in DMA_NAMES else 1) for n in sem_names}

        class Count:
            def __init__(self):
                self.start = dict(START)

            def enter(self, seg, i):
                self.seg, self.i = seg, i

            def leave(self):
                for n, v in self.seg.total.items():
                    self.start[n] += v * self.seg.times

            def at(self, stage):
                self.stage, self.own = stage, adds(stage)

            def done(self, name):
                v = self.start[name] + self.stage.upto.get(name, 0)
                if name in self.seg.total and self.seg.times > 1:
                    v = self.i * self.seg.total[name] + v
                return v

            def before(self, name):
                return self.done(name) - self.own.get(name, 0)

        class Order:
            ROOM = 512

            def __init__(self, eng, name):
                self.eng, self.sem, self.start, self.n, self.i = eng, chain_sem[name], 0, 0, None

            def enter(self, seg, i):
                self.seg, self.i, self.n = seg, i, 0

            def leave(self):
                if self.seg.times > 1:
                    assert self.n < self.ROOM, self.n
                    self.eng.nop().then_inc(self.sem, self.ROOM - self.n)
                    self.eng.wait_ge(self.sem, self.start + self.i * self.ROOM + self.ROOM)

            def left(self):
                self.start += self.ROOM * self.seg.times if self.seg.times > 1 else self.n

            def link(self, ins):
                self.n += 1
                ins.then_inc(self.sem, 1)
                v = self.start + self.n
                if self.seg is not None and self.seg.times > 1:
                    v = self.i * self.ROOM + v
                self.eng.wait_ge(self.sem, v)

        def run(eng, cnt, order, do):
            for seg in segs:
                def body(i):
                    cnt.enter(seg, i)
                    if order:
                        order.enter(seg, i)
                    for s in seg.stages:
                        f = do.get(s.kind)
                        if f:
                            cnt.at(s)
                            f(i + seg.first if seg.times > 1 else seg.first, **s.a)
                    if order:
                        order.leave()
                if seg.times > 1:
                    with eng.Fori(0, seg.times) as i:
                        body(i)
                else:
                    body(0)
                cnt.leave()
                if order:
                    order.left()

        def all_done(eng, cnt):
            def f(g):
                for n in cnt.start:
                    if cnt.start[n] > START[n]:
                        eng.wait_ge(sem[n], cnt.start[n])
            return f

        def begin(eng, names, order_sem=None):
            for n in names:
                eng.nop().then_inc(sem[n], START[n])

        PE_NAMES = [n for n in sem_names if n.startswith("full") or n in
                    ("w_used", "proj0_full", "y_full", "xt_full", "pv_done")]
        SP_NAMES = [n for n in sem_names if "_in" in n]
        ACT_NAMES = [n for n in sem_names if "_out" in n] + ["w_hi", "exp_ready", "e_rows", "y_sq", "x_sq", "x_normed", "x_hi",
                                                            "proj0_drained", "proj1_drained"]
        POOL_NAMES = ["o_rstd", "s_rstd", "y_rstd", "x_rstd"]
        DVE_NAMES = [n for n in sem_names if n not in PE_NAMES + SP_NAMES + ACT_NAMES + POOL_NAMES]

        block = ctx.enter_context(nc.Block())

        @block.sync
        def _(sp):
            c = Count()

            begin(sp, SP_NAMES)
            sp.nop().then_inc(starts_done, 1)
            sp.wait_ge(starts_done, 5)
            sp.dma_start(pt[:], page_table.rearrange("b n -> (b n)").unsqueeze(0)).then_inc(page_table_in, 16)
            sp.dma_start(eye[:], eye_d).then_inc(const_in, 16)
            with nc.allow_non_contiguous_dma("small vectors, once"):
                for n, w in enumerate((norm_pre_attn, norm_pre_ret)):
                    sp.dma_start(wpre[:, n, :], w.rearrange("(k p) -> p k", p=128)).then_inc(const_in, 16)
                sp.dma_start(subln[:], subln_w_attn.rearrange("(e p) -> p e", p=128)).then_inc(const_in, 16)
            for n, v in enumerate((lambda_q1, lambda_k1, lambda_q2, lambda_k2)):
                sp.dma_start(njunk[:, n * 128:(n + 1) * 128], v.partition_broadcast(128)).then_inc(const_in, 16)
            sp.wait_ge(page_table_in, 16)

            def stand_apart():
                if c.seg.times > 1:
                    sp.sem_inc(sp_passed, 1)

            def load_w(g, slot, w, row, cols, coef):
                sp.wait_ge(sem["w_lo"], c.before("w_lo"))
                stand_apart()
                col = bass.ds(g * coef + cols, 256) if coef else slice(cols, cols + 256)
                sp.dma_start(WR[:, slot, :, :], weights[w][:, row:row + CH, col]).then_inc(sem[f"w_in{slot}"], 16)

            def load_g(g, layer, row, kt):
                for n in ("gated_out", "gs_out") if layer == "out0" else ("gt_out0", "gt_out1"):
                    sp.wait_ge(sem[n], c.before(n))
                sp.wait_ge(sem["w_lo"], c.before("w_lo"))
                sp.dma_start(gstage[:, kt:kt + CH, :], gated[layer][:, row:row + CH, :]).then_inc(sem[f"gated_in{kt // CH}"], 16)

            def load_cache(src, ring, name, freed):
                def f(g, b, p):
                    sp.wait_ge(sem[freed(p)], c.before(freed(p)))
                    stand_apart()
                    page = sp.value_load(pt[0:1, b * PAGES + p:b * PAGES + p + 1], min_val=0, max_val=src.shape[0] - 1)
                    sp.dma_start(ring[:, p % RING[name], :],
                                 src[bass.ds(page, 1), :, bass.ds((g - 1) * 512, 512)].rearrange("a s n -> s (a n)")
                                 ).then_inc(sem[f"{name}_in{p % RING[name]}"], 16)
                return f

            def load_bias_sample(g):
                sp.wait_ge(sem["drained7"], c.before("drained7"))
                sp.wait_ge(sem["drained6"], c.before("drained6"))
                stand_apart()
                sp.dma_start(pair_row[:], bias_pairs_d[bass.ds(g - 1, 1), :, :].rearrange("a p n -> p (a n)")
                             ).then_inc(sem["bias_sample_in"], 16)

            def row_tables(g):
                sp.dma_start(dist_past[:], rows_d[:, 0:GROUP * PAGE]).then_inc(rows_in, 16)
                sp.dma_start(picks[:], rows_d[:, GROUP * PAGE:GROUP * PAGE + 32]).then_inc(rows_in, 16)

            def load_bias_prompt(g, head):
                sp.wait_ge(sem["drained5"], c.before("drained5"))
                stand_apart()
                sp.dma_start(bH[:], bias_prompt_d[bass.ds(g * 2 + head, 1), :, :].rearrange("a p n -> p (a n)")
                             ).then_inc(sem["bias_prompt_in"], 16)

            def load_head(g):
                if True:
                    sp.wait_ge(sem["drained4"], c.before("drained4"))
                    sp.wait_ge(sem["drained5"], c.before("drained5"))
                    sp.wait_ge(sem["drained6"], c.before("drained6"))
                    sp.wait_ge(sem["drained7"], c.before("drained7"))
                stand_apart()
                sp.dma_start(hc[:], heads_d[bass.ds(g, 1), :, :].rearrange("a p n -> p (a n)")).then_inc(sem["head_in"], 16)

            def load_rope(g):
                sp.dma_start(rope[:], rope_d).then_inc(rope_in, 16)

            def load_state(g, b):
                for n in ("full6", "drained4", "drained5", "full5"):
                    sp.wait_ge(sem[n], c.before(n))
                    stand_apart()
                sp.dma_start(Sin[:, b % 3, :].rearrange("p (e v) -> p e v", e=2),
                             st_in[bass.ds(g + b * HEADS, 1), :, :, :].rearrange("a p e v -> p (a e) v")
                             ).then_inc(sem[f"state_in{b % 3}"], 16)

            def load_x(t, src):
                R = TILES[t][1]
                sp.dma_start(xt[0:R, t % 2, :], src if src is not None else (xp[t * 128:t * 128 + R, :] if t < 4 else xs)
                             ).then_inc(sem[f"x_in{t % 2}"], 16)

            def y_tile(g, t, stage):
                R = TILES[t][1]
                if t == 0:
                    for n in ("proj1_drained", "x_sum", "w_lo"):
                        sp.wait_ge(sem[n], c.before(n))
                    sp.dma_start(wpost[:], (norm_post_attn, norm_post_ret)[stage - 1].partition_broadcast(128)).then_inc(wpost_in, 16)
                sp.wait_ge(sem[f"x_out{t % 2}"], c.before(f"x_out{t % 2}"))
                sp.wait_ge(sem["x_normed"], c.before("x_normed"))
                load_x(t, x1_d[t * 128:t * 128 + R, :] if stage == 2 else None)

            def x_tile(g, t, stage):
                if not stage:
                    if t > 1:
                        sp.wait_ge(sem["x_normed"], c.before("x_normed") - 1)
                    load_x(t, None)

            run(sp, c, None, dict(relay_area=all_done(sp, c), load_w=load_w, load_g=load_g, load_k=load_cache(ck, Kr, "k", lambda p: f"full{4 + p % 2}"),
                                  load_v=load_cache(cv, Vr, "v", lambda p: "pv_done"), load_bias_sample=load_bias_sample,
                                  load_bias_prompt=load_bias_prompt, load_head=load_head, load_state=load_state,
                                  y_tile=y_tile, x_tile=x_tile, load_rope=load_rope, row_tables=row_tables))

        @block.tensor
        def _(pe):
            c = Count()

            begin(pe, PE_NAMES)
            pe.nop().then_inc(starts_done, 1)
            pe.wait_ge(starts_done, 5)
            pe.wait_ge(const_in, 8 * 16)
            pe.wait_ge(setup_done, 2)

            def mm(out, a, b, start=True, stop=True):
                return nc.tensor.matmul(out, a, b, start=start, stop=stop, skip_group_check=True)

            def tr(out, a, n=128):
                return nc.tensor.matmul(out, a, ident[0:n, 0:n], start=True, stop=True, is_transpose=True, skip_group_check=True)

            def project(g, i):
                chunk, cb, k = i // 8, (i // 4) % 2, i % 4
                slot, kt = chunk % 2, chunk * CH + k
                if i % 8 == 0:
                    pe.wait_ge(sem["w_lo"], c.before("w_lo"))
                if i == 0:
                    pe.wait_ge(sem["x_lo"], c.before("x_lo"))
                if i in (0, 4):
                    pe.wait_ge(sem[f"proj{cb}_drained"], c.before(f"proj{cb}_drained"))
                w = slice(cb * 128, cb * 128 + 128)
                for n, (a, x) in enumerate(((WH, XH), (WH, XL), (WL, XH))):
                    for half in range(2):
                        last = mm(bank[2 * cb + half][:, 0:HALF], a[:, slot, k, w], x[:, kt, half * HALF:(half + 1) * HALF],
                                  start=kt == 0 and n == 0, stop=kt == KT - 1 and n == 2)
                if i == 27:
                    last.then_inc(sem["proj0_full"], 1)
                elif i % 8 == 7:
                    last.then_inc(sem["w_used"], 1)

            def scores(g, hp, qb, back):
                n = (qb + 1) * 128
                for d in ("proj0_drained", "proj1_drained"):
                    pe.wait_ge(sem[d], c.before(d))
                for cc in range(2):
                    pe.wait_ge(sem[f"drained{4 + cc}"], c.before(f"drained{4 + cc}"))
                    mm(bank[4 + cc][:, 0:n], qT[hp][:, cc, qb * 128:(qb + 1) * 128], kT[hp][:, cc, 0:n]
                       ).then_inc(sem[f"full{4 + cc}"], 1)

            def free7():
                pe.wait_ge(sem["drained7"], c.before("drained7"))

            def p_transpose(g, hp, qb, back):
                pe.wait_ge(sem["p_ready"], c.before("p_ready"))
                free7()
                for k in range(qb + 1):
                    last = tr(bank[7][:, k * 128:(k + 1) * 128], sc[:, 0, k * 128:(k + 1) * 128])
                last.then_inc(sem["full7"], 1)

            def pv(g, hp, qb, back):
                free7()
                for k in range(qb + 1):
                    last = mm(bank[7][:, 0:256], pT[:, k * 128:(k + 1) * 128], vn[hp][:, k, :], start=k == 0, stop=k == qb)
                last.then_inc(sem["full7"], 1)

            def o_transpose(g, hp, qb, back):
                pe.wait_ge(sem["o_normed"], c.before("o_normed"))
                free7()
                for e in range(2):
                    last = tr(bank[7][:, e * 128:(e + 1) * 128], oP[:, e * 128:(e + 1) * 128])
                last.then_inc(sem["full7"], 1)

            def natural(g, what, hh, j):
                for d in ("proj0_drained", "proj1_drained"):
                    pe.wait_ge(sem[d], c.before(d))
                free7()
                if j == 2:
                    pe.sem_inc(pe_passed, 1)
                src = {"k": kT[hh], "v": vT, "r": rvT}[what]
                for t, R in TILES[2 * j:2 * j + 2]:
                    for cb in range(2):
                        o = (t % 2) * 256 + cb * 128
                        last = tr(bank[7][0:R, o:o + 128], src[:, cb, t * 128:t * 128 + R])
                last.then_inc(sem["full7"], 1)

            def page(g, b, p):
                n = 4 + p % 2
                pe.wait_ge(sem[f"k_in{p % RING['k']}"], c.before(f"k_in{p % RING['k']}"))
                pe.wait_ge(sem[f"drained{n}"], c.before(f"drained{n}"))
                for j in range(4):
                    last = tr(bank[n][:, j * 128:(j + 1) * 128], Kr[:, p % RING["k"], j * 128:(j + 1) * 128])
                last.then_inc(sem[f"full{n}"], 1)

            def qk(g, b, group):
                for n in (4, 5):
                    pe.wait_ge(sem[f"drained{n}"], c.before(f"drained{n}"))
                pe.wait_ge(sem["drained6"], c.before("drained6"))
                pe.wait_ge(sem["q_placed"], c.before("q_placed"))
                for j in range(4):
                    last = mm(bank[6][0:32, :], qrow[:, j * 32:(j + 1) * 32], KTs[:, j, :], start=j == 0, stop=j == 3)
                last.then_inc(sem["full6"], 1)

            def soft_new(g, b):
                free7()
                for j in range(4):
                    last = mm(bank[7][0:32, 0:SMP], qrow[:, j * 32:(j + 1) * 32], kS[:, j, :], start=j == 0, stop=j == 3)
                last.then_inc(sem["full7"], 1)

            def e_transpose(g, b):
                pe.wait_ge(sem["drained4"], c.before("drained4"))
                pe.wait_ge(sem["drained5"], c.before("drained5"))
                pe.wait_ge(sem["e_rows"], c.before("e_rows"))
                pe.sem_inc(pe_passed, 1)
                for p in range(PAGES):
                    last = tr(bank[4][:, p * 32:(p + 1) * 32], sS[:, p * 128:(p + 1) * 128], 32)
                last.then_inc(sem["full4"], 1)
                tr(bank[5][0:SMP, 0:32], sN[:], 32).then_inc(sem["full5"], 1)

            def value(g, b, p):
                if p == 0:
                    pe.wait_ge(sem["drained4"], c.before("drained4"))
                    pe.wait_ge(sem["drained6"], c.before("drained6"))
                pe.wait_ge(sem[f"v_in{p % RING['v']}"], c.before(f"v_in{p % RING['v']}"))
                mm(bank[6][0:32, :], e_all[:, p, :], Vr[:, p % RING["v"], :], start=p == 0, stop=False).then_inc(sem["pv_done"], 1)

            def value_new(g, b):
                pe.wait_ge(sem["drained5"], c.before("drained5"))
                pe.sem_inc(pe_passed, 1)
                mm(bank[6][0:32, :], e_new[:], vS[0:SMP, :], start=False).then_inc(sem["full6"], 1)

            def mix(g, b):
                pe.wait_ge(sem["drained6"], c.before("drained6"))
                pe.wait_ge(sem["mix_ready"], c.before("mix_ready"))
                free7()
                for k in range(4):
                    h = k // 2
                    last = mm(bank[7][:, k * NQ:(k + 1) * NQ], sS[:, k * 128:(k + 1) * 128], mixw[:, h * NQ:(h + 1) * NQ])
                last.then_inc(sem["full7"], 1)

            def sample_end(g):
                pe.wait_ge(sem["sq_ready"], c.done("sq_ready"))
                free7()
                mm(bank[7][:, 0:256], ones, oQ[:].rearrange("p a b -> p (a b)")).then_inc(sem["full7"], 1)

            def ret_scores(g, c_):
                lo = c_ * 128
                pe.wait_ge(sem["rotated"], c.before("rotated"))
                pe.wait_ge(sem["drained4"], c.before("drained4"))
                for e in range(2):
                    last = mm(bank[4][:, 0:128], rkT[:, e, lo:lo + 128], rqT[:, e, lo:lo + 128], start=e == 0, stop=e == 1)
                last.then_inc(sem["full4"], 1)
                pe.wait_ge(sem["drained5"], c.before("drained5"))
                for e in range(2):
                    last = tr(bank[5][:, e * 128:(e + 1) * 128], rkT[:, e, lo:lo + 128])
                last.then_inc(sem["full5"], 1)

            def ret_out(g, c_):
                for n in ("drained4", "qd_ready", "drained6", "drained7"):
                    pe.wait_ge(sem[n], c.before(n))
                mm(bank[6][:, :], sT[:], rvn[:, c_, :], start=True, stop=c_ == 0)
                if c_ == 0:
                    pe.wait_ge(sem["drained5"], c.before("drained5"))
                last = None
                if c_:
                    for e in range(2):
                        last = mm(bank[6][:, :], qd[:, e, :], Sp[:, e, :], start=False, stop=e == 1)
                    last.then_inc(sem["full6"], 1)

            def ret_out0(g, c_):
                for n in ("drained4", "qd_ready", "drained6", "drained7"):
                    pe.wait_ge(sem[n], c.before(n))
                mm(bank[6][:, :], sT[:], rvn[:, c_, :]).then_inc(sem["full6"], 1)

            def ret_state(g, c_):
                for e in range(2):
                    pe.wait_ge(sem[f"drained{4 + e}"], c.before(f"drained{4 + e}"))
                    if e == 0:
                        pe.wait_ge(sem["drained5"], c.before("drained5"))
                    mm(bank[4 + e][:, :], kd[:, e * 128:(e + 1) * 128], rvn[:, c_, :]).then_inc(sem[f"full{4 + e}"], 1)

            def rs_scores(g):
                pe.wait_ge(sem["drained4"], c.before("drained4"))
                pe.sem_inc(pe_passed, 1)
                for e in range(2):
                    last = mm(bank[4][0:SMP, 0:SMP], rkT[:, e, SEQ:T], rqT[:, e, SEQ:T], start=e == 0, stop=e == 1)
                last.then_inc(sem["full4"], 1)
                pe.wait_ge(sem["drained5"], c.before("drained5"))
                pe.sem_inc(pe_passed, 1)
                for e in range(2):
                    last = tr(bank[5][0:SMP, e * 128:(e + 1) * 128], rkT[:, e, SEQ:T])
                last.then_inc(sem["full5"], 1)

            def rs_intra(g):
                for n in ("drained4", "drained5", "drained6", "qd_ready"):
                    pe.wait_ge(sem[n], c.before(n))
                pe.sem_inc(pe_passed, 1)
                mm(bank[6][0:SMP, :], sT[0:SMP, 0:SMP], rvn[0:SMP, 4, :], start=True, stop=False)

            def rs_state(g, b):
                pe.wait_ge(sem[f"state_in{b % 3}"], c.before(f"state_in{b % 3}"))
                pe.sem_inc(pe_passed, 1)
                for e in range(2):
                    mm(bank[6][0:SMP, :], qz[:, e, b * SMP:(b + 1) * SMP], Sin[:, b % 3, e * 512:(e + 1) * 512],
                       start=False, stop=b == NB - 1 and e == 1)
                for e in range(2):
                    pe.wait_ge(sem[f"drained{4 + e}"], c.before(f"drained{4 + e}"))
                    mm(bank[4 + e][:, :], kz[:, b, e * 128:(e + 1) * 128], rvn[0:SMP, 4, :]).then_inc(sem[f"full{4 + e}"], 1)

            def rs_out(g):
                pe.wait_ge(sem["full5"], c.before("full5"))
                pe.nop().then_inc(sem["full6"], 1)

            def gate(g, t):
                n, R = 4 + t % 2, TILES[t][1]
                if t == 0:
                    pe.wait_ge(sem["o_normed"], c.before("o_normed"))
                pe.wait_ge(sem[f"drained{n}"], c.before(f"drained{n}"))
                pe.sem_inc(pe_passed, 1)
                for j in range(4):
                    last = tr(bank[n][:, j * 128:j * 128 + R], oN[0:R, t, j * 128:(j + 1) * 128], R)
                last.then_inc(sem[f"full{n}"], 1)

            def y_tile(g, t, stage):
                R = TILES[t][1]
                for n in ("proj0_drained", "proj1_drained", "y_used"):
                    pe.wait_ge(sem[n], c.before(n))
                for j in range(KT):
                    last = tr(bank[j // 4][0:R, (j % 4) * 128:(j % 4) * 128 + 128], yT[:, j, t * 128:t * 128 + R])
                last.then_inc(sem["y_full"], 1)

            def x_tile(g, t, stage):
                R = TILES[t][1]
                pe.wait_ge(sem["x_normed"], c.done("x_normed"))
                pe.wait_ge(sem["x_lo"], c.before("x_lo"))
                for j in range(KT):
                    last = tr(bank[4 + j // 4][:, (j % 4) * 128:(j % 4) * 128 + R], yn[0:R, t % 2, j * 128:(j + 1) * 128], R)
                last.then_inc(sem["xt_full"], 1)

            run(pe, c, None, dict(project=project, scores=scores, p_transpose=p_transpose, pv=pv, o_transpose=o_transpose,
                                  natural=natural, page=page, qk=qk, soft_new=soft_new, e_transpose=e_transpose, mix=mix, value=value, value_new=value_new, sample_end=sample_end,
                                  ret_scores=lambda g, c: ret_scores(g, c),
                                  ret_out=lambda g, c: (ret_out if c else ret_out0)(g, c),
                                  ret_state=lambda g, c: ret_state(g, c), rs_scores=rs_scores, rs_intra=rs_intra,
                                  rs_state=rs_state, rs_out=rs_out, gate=gate, y_tile=y_tile, x_tile=x_tile))

        @block.scalar
        def _(act):
            c, o = Count(), Order(act, "act")

            def copy(out, in_, scale=1.0):
                return nc.scalar.activation(out, in_, ACT.Copy, scale=scale)

            begin(act, ACT_NAMES)
            act.nop().then_inc(starts_done, 1)
            act.wait_ge(starts_done, 5)
            act.wait_ge(lam_dot, 1)
            nc.scalar.activation(small[:, 2:4], small[:, 0:2], ACT.Exp).then_inc(lam_exp, 1)

            def split_w(g, slot):
                act.wait_ge(sem[f"w_in{slot}"], c.before(f"w_in{slot}"))
                act.wait_ge(sem["w_used"], c.before("w_used"))
                copy(WH[:, slot, :, :], WR[:, slot, :, :]).then_inc(sem["w_hi"], 1)
                act.wait_ge(sem["w_hi"], c.done("w_hi"))

            def split_g(g, kt):
                act.wait_ge(sem[f"gated_in{kt // CH}"], c.before(f"gated_in{kt // CH}"))
                act.wait_ge(sem["w_used"], c.before("w_used"))
                copy(XH[:, kt, :], gstage[:, kt, :]).then_inc(sem["w_hi"], 1)
                act.wait_ge(sem["w_hi"], c.done("w_hi"))

            def evacuate(g, cb, kind, hh):
                full = "w_used" if cb else "proj0_full"
                act.wait_ge(sem[full], c.before(full))
                if kind == "+":
                    return
                f, extra = ACT.Copy, None
                if kind == "g":
                    act.wait_ge(sem["drained7"], c.before("drained7"))
                    act.wait_ge(sem["carried"], c.before("carried"))
                    dst, f, extra = sg[:, cb, :], ACT.Silu, sgN[:, hh * 2 + cb, :]
                elif kind == "gr":
                    for n in ("drained4", "drained5"):
                        act.wait_ge(sem[n], c.before(n))
                    dst, f = rsg[:, hh * 2 + cb, :], ACT.Silu
                elif kind in ("q", "k"):
                    act.wait_ge(sem["full7"], c.before("full7"))
                    act.wait_ge(sem["carried"], c.before("carried"))
                    act.wait_ge(sem["full4"], c.before("full4"))
                    act.wait_ge(sem["full5"], c.before("full5"))
                    dst = (qT if kind == "q" else kT)[hh][:, cb, :]
                elif kind == "v":
                    act.wait_ge(sem["full7"], c.before("full7"))
                    dst = vT[:, cb, :]
                elif kind in ("qr", "kr"):
                    act.wait_ge(sem["rotated"], c.before("rotated"))
                    dst = raw[:, cb, :]
                elif kind == "vr":
                    act.wait_ge(sem["full7"], c.before("full7"))
                    dst = rvT[:, cb, :]
                else:
                    for n in ("drained4", "drained5", "drained6", "drained7"):
                        act.wait_ge(sem[n], c.before(n))
                    dst = yT[:, hh * 2 + cb, :]
                o.link(nc.scalar.activation(dst[:, 0:HALF], bank[2 * cb][:, 0:HALF], f))
                last = nc.scalar.activation(dst[:, HALF:T], bank[2 * cb + 1][:, 0:HALF], f)
                if extra is not None:
                    o.link(last)
                    last = copy(extra, dst[:, SEQ:T])
                last.then_inc(sem[f"proj{cb}_drained"], 1)
                act.wait_ge(sem[f"proj{cb}_drained"], c.done(f"proj{cb}_drained"))

            def scores(g, hp, qb, back):
                n = (qb + 1) * 128
                act.wait_ge(sem["max_ready"], c.done("max_ready"))
                for cc in range(2):
                    ins = nc.scalar.activation(sc[:, cc, 0:n], sc[:, cc, 0:n], ACT.Exp, bias=pst[:, cc:cc + 1],
                                               accum_out=pst[:, 2 + cc:3 + cc])
                    if cc:
                        ins.then_inc(sem["exp_ready"], 1)
                        act.wait_ge(sem["exp_ready"], c.done("exp_ready"))
                    else:
                        o.link(ins)

            def p_transpose(g, hp, qb, back):
                n = (qb + 1) * 128
                act.wait_ge(sem["full7"], c.done("full7"))
                copy(pT[:, 0:n], bank[7][:, 0:n]).then_inc(sem["drained7"], 1)
                act.wait_ge(sem["drained7"], c.done("drained7"))

            def natural(g, what, hh, j):
                act.wait_ge(sem["full7"], c.done("full7"))
                if what == "r":
                    for n in ("full4", "full5", "full6"):
                        act.wait_ge(sem[n], c.before(n))
                elif j == 0:
                    act.wait_ge(sem["natural_out"], c.before("natural_out"))
                dst = {"k": kn, "v": vn[hh], "r": rvn}[what]
                cols = slice(hh * 256, hh * 256 + 256) if what == "r" else slice(0, 256)
                if j < 2:
                    ins = copy(dst[:, 2 * j:2 * j + 2, cols], bank[7][:, :].rearrange("p (a b) -> p a b", a=2))
                else:
                    ins = copy(dst[0:SMP, 4, cols], bank[7][0:SMP, 0:256])
                ins.then_inc(sem["drained7"], 1)
                act.wait_ge(sem["drained7"], c.done("drained7"))

            def store_natural(g, what, hh):
                src = {"k": kn, "v": vn[hh]}[what]
                dp, ds = natural_out[what]
                col = bass.ds(g * 512 + hh * 256, 256)
                act.dma_start(dp[:, :, col], src[:, 0:4, :]).then_inc(sem["natural_out"], 16)
                act.dma_start(ds[:, col], src[0:SMP, 4, :]).then_inc(sem["natural_out"], 16)

            def store_gated(g, hp, qb, back):
                act.wait_ge(sem["drained7"], c.before("drained7"))
                row = g * 512 + back * 256
                act.dma_start(gated0_d[bass.ds(row, 256), qb * 128:(qb + 1) * 128].rearrange("(e p) t -> p e t", p=128), gP[:]
                              ).then_inc(sem["gated_out"], 16)

            def page(g, b, p):
                if p % 2 == 0:
                    act.wait_ge(sem["full4"], c.done("full4"))
                    act.wait_ge(sem["full6"], c.before("full6"))
                    copy(KTs[:, :, (p % GROUP) * 128:(p % GROUP + 1) * 128], bank[4][:, :].rearrange("p (j s) -> p j s", j=4)
                         ).then_inc(sem["drained4"], 1)
                    act.wait_ge(sem["drained4"], c.done("drained4"))

            def soft_exp(g, b):
                act.wait_ge(sem["rows_ready"], c.before("rows_ready"))
                for n in range(PAGES // GROUP):
                    part = sS[:, n * 512:(n + 1) * 512]
                    o.link(nc.scalar.activation(part, part, ACT.Exp, bias=ebias[:, n:n + 1], accum_out=lsum[:, n:n + 1]))
                nc.scalar.activation(sN[:], sN[:], ACT.Exp, bias=ebias[:, 4:5], accum_out=lsum[:, 4:5]).then_inc(sem["e_rows"], 1)
                act.wait_ge(sem["e_rows"], c.done("e_rows"))

            def e_transpose(g, b):
                act.wait_ge(sem["full4"], c.done("full4"))
                act.wait_ge(sem["pv_done"], c.before("pv_done"))
                copy(e_all[:].rearrange("p a b -> p (a b)"), bank[4][:, :]).then_inc(sem["drained4"], 1)
                act.wait_ge(sem["drained4"], c.done("drained4"))

            def value_new(g, b):
                act.wait_ge(sem["full6"], c.done("full6"))
                act.wait_ge(sem["full5"], c.before("full5"))
                copy(sS[:, 0:512], bank[6][0:32, :]).then_inc(sem["drained6"], 1)
                act.wait_ge(sem["drained6"], c.done("drained6"))

            def store_sample(g):
                act.wait_ge(sem["gs_ready"], c.before("gs_ready"))
                act.dma_start(gated0_d[bass.ds(g * 512 - 512, 512), SEQ:T].rearrange("(k p) t -> p k t", p=128), oQ[:]
                              ).then_inc(sem["gs_out"], 16)

            def ret_scores(g, c_):
                act.wait_ge(sem["full5"], c.done("full5"))
                copy(kd[:], bank[5][:, 0:256], scale=hc[:, 392:393]).then_inc(sem["drained5"], 1)
                act.wait_ge(sem["drained5"], c.done("drained5"))

            def ret_out(g, c_):
                act.wait_ge(sem["full6"], c.done("full6"))
                act.wait_ge(sem["full4"], c.before("full4"))
                copy(oN[:, c_, :], bank[6][:, :]).then_inc(sem["drained6"], 1)
                act.wait_ge(sem["drained6"], c.done("drained6"))

            def rs_out(g):
                act.wait_ge(sem["full6"], c.done("full6"))
                copy(oN[0:SMP, 4, :], bank[6][0:SMP, :]).then_inc(sem["drained6"], 1)
                act.wait_ge(sem["drained6"], c.done("drained6"))

            def store_state_p(g):
                act.wait_ge(sem["drained4"], c.before("drained4"))
                act.wait_ge(sem["drained5"], c.before("drained5"))
                act.dma_start(sp_out[bass.ds(g, 1), :, :, :].rearrange("a p e v -> p (a e) v"), Sp[:]).then_inc(sem["sp_out"], 16)

            def store_state(g, b):
                act.wait_ge(sem["drained4"], c.before("drained4"))
                act.wait_ge(sem["drained5"], c.before("drained5"))
                act.dma_start(st_out[bass.ds(g + b * HEADS, 1), :, :, :].rearrange("a p e v -> p (a e) v"),
                              Sout[:, b % 2, :].rearrange("p (e v) -> p e v", e=2)).then_inc(sem[f"state_out{b % 2}"], 16)

            def store_ret(g, t):
                n, R = 4 + t % 2, TILES[t][1]
                act.wait_ge(sem[f"drained{n}"], c.before(f"drained{n}"))
                act.dma_start(gated1_d[bass.ds(g * 512, 512), t * 128:t * 128 + R].rearrange("(k p) t -> p k t", p=128),
                              gt[:, t % 2, :].rearrange("p (k t) -> p k t", k=4)[:, :, 0:R]).then_inc(sem[f"gt_out{t % 2}"], 16)

            def y_tile(g, t, stage):
                R = TILES[t][1]
                act.wait_ge(sem["y_full"], c.done("y_full"))
                nc.scalar.activation(njunk[0:R, :], low[0:R, :, :].rearrange("p a b -> p (a b)"), ACT.Square,
                                     accum_out=nst[0:R, t % 2, 0:1]).then_inc(sem["y_sq"], 1)
                act.wait_ge(sem["y_sq"], c.done("y_sq"))

            def x_tile(g, t, stage):
                R = TILES[t][1]
                if stage:
                    act.wait_ge(sem["x_sum"], c.before("x_sum"))
                else:
                    act.wait_ge(sem[f"x_in{t % 2}"], c.done(f"x_in{t % 2}"))
                nc.scalar.activation(njunk[0:R, :], xt[0:R, t % 2, :], ACT.Square, accum_out=nst[0:R, t % 2, 2:3]
                                     ).then_inc(sem["x_sq"], 1)
                act.wait_ge(sem["x_rstd"], c.done("x_rstd"))
                act.wait_ge(sem["xt_full"], c.before("xt_full"))
                copy(yn[0:R, t % 2, :], xt[0:R, t % 2, :], scale=nst[0:R, t % 2, 3:4]).then_inc(sem["x_normed"], 1)
                act.wait_ge(sem["x_normed"], c.done("x_normed"))
                act.wait_ge(sem["xt_full"], c.done("xt_full"))
                for j in range(KT):
                    ins = copy(XH[:, j, t * 128:t * 128 + R], bank[4 + j // 4][:, (j % 4) * 128:(j % 4) * 128 + R],
                               scale=wpre[:, stage, j:j + 1])
                    if j % 4 == 3:
                        ins.then_inc(sem["x_hi"], 1)
                act.wait_ge(sem["x_hi"], c.done("x_hi"))

            def store_x(g, t, stage):
                R = TILES[t][1]
                act.wait_ge(sem["x_sum"], c.before("x_sum") - (1 if t < 4 else 0))
                dst = x1_d[t * 128:t * 128 + R, :] if stage == 1 else (yp[t * 128:t * 128 + R, :] if t < 4 else ys)
                act.dma_start(dst, xt[0:R, t % 2, :]).then_inc(sem[f"x_out{t % 2}"], 16)

            run(act, c, o, dict(relay_area=all_done(act, c), split_w=split_w, split_g=split_g, evacuate=evacuate, scores=scores, p_transpose=p_transpose,
                                natural=natural, store_natural=store_natural, store_gated=store_gated, page=page,
                                soft_exp=soft_exp, e_transpose=e_transpose, value_new=value_new, store_sample=store_sample,
                                ret_scores=lambda g, c: ret_scores(g, c), ret_out=lambda g, c: ret_out(g, c),
                                rs_out=rs_out, store_state_p=store_state_p, store_state=store_state, store_ret=store_ret,
                                y_tile=y_tile, x_tile=x_tile, store_x=store_x))
            for n in sem_names:
                if "_out" in n:
                    act.wait_ge(sem[n], c.start[n])

        @block.vector
        def _(dve):
            c, o = Count(), Order(dve, "dve")
            v = nc.vector

            def variance(ss, n):
                return v.tensor_scalar(ss, ss, 1.0 / n, EPS, MUL, ADD)

            begin(dve, DVE_NAMES)
            dve.nop().then_inc(starts_done, 1)
            dve.wait_ge(starts_done, 5)
            o.seg = None
            dve.wait_ge(const_in, 8 * 16)
            for n in range(2):
                o.link(v.tensor_tensor_reduce(out=njunk[:, 512:640], in0=njunk[:, n * 256:n * 256 + 128],
                                              in1=njunk[:, n * 256 + 128:n * 256 + 256], scale=1.0, scalar=0.0, op0=MUL, op1=ADD,
                                              accum_out=small[:, n:n + 1]))
            v.memset(power[:], -0.5).then_inc(lam_dot, 1)
            dve.wait_ge(lam_exp, 1)
            o.link(v.tensor_tensor(lam_neg[:], small[:, 3:4], small[:, 2:3], SUB))
            v.tensor_scalar(lam_neg[:], lam_neg[:], -LAMBDA_INIT, None, ADD).then_inc(setup_done, 1)
            v.tensor_scalar(subln[:], subln[:], 1.0 - LAMBDA_INIT, None, MUL).then_inc(setup_done, 1)
            dve.wait_ge(setup_done, 2)
            o.start = o.n

            def row_tables(g):
                dve.wait_ge(rows_in, 32)
                o.link(v.scalar_tensor_tensor(out=pick_lam[:], in0=picks[:, 16:32], scalar=lam_neg[0:32, :], in1=picks[:, 0:16],
                                              op0=MUL, op1=ADD))
                o.link(v.memset(qrow[:], 0.0))

            def split_w(g, slot):
                dve.wait_ge(sem["w_hi"], c.done("w_hi"))
                v.tensor_tensor(WL[:, slot, :, :], WR[:, slot, :, :], WH[:, slot, :, :].bitcast(f32), SUB).then_inc(sem["w_lo"], 1)
                dve.wait_ge(sem["w_lo"], c.done("w_lo"))

            def split_g(g, kt):
                dve.wait_ge(sem["w_hi"], c.done("w_hi"))
                v.tensor_tensor(XL[:, kt, :], gstage[:, kt, :], XH[:, kt, :].bitcast(f32), SUB).then_inc(sem["w_lo"], 1)
                dve.wait_ge(sem["w_lo"], c.done("w_lo"))

            def evacuate(g, cb, kind, hh):
                if kind == "+":
                    full = "w_used" if cb else "proj0_full"
                    dve.wait_ge(sem[full], c.before(full))
                    dst = yT[:, hh * 2 + cb, :]
                    o.link(v.tensor_tensor(dst[:, 0:HALF], bank[2 * cb][:, 0:HALF], dst[:, 0:HALF], ADD))
                    v.tensor_tensor(dst[:, HALF:T], bank[2 * cb + 1][:, 0:HALF], dst[:, HALF:T], ADD).then_inc(sem[f"proj{cb}_drained"], 1)
                    dve.wait_ge(sem[f"proj{cb}_drained"], c.done(f"proj{cb}_drained"))

            def scores(g, hp, qb, back):
                n = (qb + 1) * 128
                dve.wait_ge(sem["bias_prompt_in"], c.before("bias_prompt_in"))
                dve.wait_ge(sem["full7"], c.before("full7"))
                for cc in range(2):
                    dve.wait_ge(sem[f"full{4 + cc}"], c.done(f"full{4 + cc}"))
                    v.scalar_tensor_tensor(out=sc[:, cc, 0:n], in0=bank[4 + cc][:, 0:n], scalar=SCALE,
                                           in1=bH[:, 384 - qb * 128:512], op0=MUL, op1=ADD).then_inc(sem[f"drained{4 + cc}"], 1)
                    dve.wait_ge(sem[f"drained{4 + cc}"], c.done(f"drained{4 + cc}"))
                for cc in range(2):
                    ins = v.reduce_max(pst[:, cc:cc + 1], sc[:, cc, 0:n], AX.X, negate=True)
                    if cc:
                        ins.then_inc(sem["max_ready"], 1)
                        dve.wait_ge(sem["max_ready"], c.done("max_ready"))
                    else:
                        o.link(ins)
                dve.wait_ge(sem["exp_ready"], c.done("exp_ready"))
                o.link(v.reciprocal(pst[:, 4:6], pst[:, 2:4]))
                o.link(v.tensor_scalar(pst[:, 5:6], pst[:, 5:6], lam_neg[:], None, MUL))
                o.link(v.tensor_scalar(sc[:, 0, 0:n], sc[:, 0, 0:n], pst[:, 4:5], None, MUL))
                v.scalar_tensor_tensor(out=sc[:, 0, 0:n], in0=sc[:, 1, 0:n], scalar=pst[:, 5:6], in1=sc[:, 0, 0:n],
                                       op0=MUL, op1=ADD).then_inc(sem["p_ready"], 1)
                dve.wait_ge(sem["p_ready"], c.done("p_ready"))

            def pv(g, hp, qb, back):
                dve.wait_ge(sem["full7"], c.done("full7"))
                v.tensor_copy(oP[:], bank[7][:, 0:256]).then_inc(sem["drained7"], 1)
                dve.wait_ge(sem["drained7"], c.done("drained7"))
                o.link(v.tensor_tensor_reduce(out=junk[:], in0=oP[:], in1=oP[:], scale=1.0, scalar=0.0, op0=MUL, op1=ADD,
                                              accum_out=pst[:, 6:7]))
                variance(pst[:, 6:7], 256).then_inc(sem["o_var"], 1)
                dve.wait_ge(sem["o_var"], c.done("o_var"))
                dve.wait_ge(sem["o_rstd"], c.done("o_rstd"))
                v.tensor_scalar(oP[:], oP[:], pst[:, 7:8], None, MUL).then_inc(sem["o_normed"], 1)
                dve.wait_ge(sem["o_normed"], c.done("o_normed"))

            def o_transpose(g, hp, qb, back):
                dve.wait_ge(sem["full7"], c.done("full7"))
                dve.wait_ge(sem["proj0_drained"], c.before("proj0_drained"))
                dve.wait_ge(sem["proj1_drained"], c.before("proj1_drained"))
                dve.wait_ge(sem["gated_out"], c.before("gated_out"))
                for e in range(2):
                    ins = v.scalar_tensor_tensor(out=gP[:, e, :], in0=bank[7][:, e * 128:(e + 1) * 128], scalar=subln[:, e:e + 1],
                                                 in1=sg[:, e, qb * 128:(qb + 1) * 128], op0=MUL, op1=MUL)
                    if e:
                        ins.then_inc(sem["drained7"], 1)
                        dve.wait_ge(sem["drained7"], c.done("drained7"))
                    else:
                        o.link(ins)

            def place_q(g, b):
                dve.wait_ge(sem["carried"], c.before("carried"))
                dve.wait_ge(sem["full7"], c.before("full7"))
                dve.wait_ge(sem["full6"], c.before("full6"))
                v.tensor_scalar(qrow[:].rearrange("p (j r) -> p j r", r=40)[:, :, 0:NQ], qS[:, :, b * NQ:(b + 1) * NQ], SCALE, None,
                                MUL).then_inc(sem["q_placed"], 1)
                dve.wait_ge(sem["q_placed"], c.done("q_placed"))

            def page(g, b, p):
                if p % 2:
                    dve.wait_ge(sem["full5"], c.done("full5"))
                    dve.wait_ge(sem["full6"], c.before("full6"))
                    v.tensor_copy(KTs[:, :, (p % GROUP) * 128:(p % GROUP + 1) * 128], bank[5][:, :].rearrange("p (j s) -> p j s", j=4)
                                  ).then_inc(sem["drained5"], 1)
                    dve.wait_ge(sem["drained5"], c.done("drained5"))

            def qk(g, b, group):
                cols = slice(group * 512, (group + 1) * 512)
                dve.wait_ge(sem["full6"], c.done("full6"))
                dve.wait_ge(sem["bias_sample_in"], c.before("bias_sample_in"))
                v.scalar_tensor_tensor(out=sS[:, cols], in0=dist_past[:], scalar=pair_row[:, 0:1], in1=bank[6][0:32, :],
                                       op0=MUL, op1=ADD).then_inc(sem["drained6"], 1)
                dve.wait_ge(sem["drained6"], c.done("drained6"))
                o.link(v.reduce_max(gmax[:, group:group + 1], sS[:, cols], AX.X))

            def soft_new(g, b):
                dve.wait_ge(sem["full7"], c.done("full7"))
                at = NPAIR + b * SMP
                v.tensor_tensor(sN[:], bank[7][0:32, 0:SMP], pair_row[:, at:at + SMP], ADD).then_inc(sem["drained7"], 1)
                dve.wait_ge(sem["drained7"], c.done("drained7"))
                o.link(v.reduce_max(gmax[:, 4:5], sN[:], AX.X))
                o.link(v.tensor_tensor(gmax[:], gmax[:], pair_row[:, 1:NPAIR], ADD))
                o.link(v.reduce_max(row1[:, 0:1], gmax[:], AX.X, negate=True))
                v.tensor_scalar(ebias[:], pair_row[:, 1:NPAIR], row1[:, 0:1], None, ADD).then_inc(sem["rows_ready"], 1)
                dve.wait_ge(sem["rows_ready"], c.done("rows_ready"))

            def e_transpose(g, b):
                dve.wait_ge(sem["full5"], c.done("full5"))
                v.tensor_copy(e_new[:], bank[5][0:SMP, 0:32]).then_inc(sem["drained5"], 1)
                dve.wait_ge(sem["drained5"], c.done("drained5"))

            def soft_exp(g, b):
                dve.wait_ge(sem["e_rows"], c.done("e_rows"))
                o.link(v.reduce_sum(row1[:, 0:1], lsum[:], AX.X))
                o.link(v.reciprocal(row1[:, 1:2], row1[:, 0:1]))
                v.tensor_scalar(mixw[:], pick_lam[:], row1[:, 1:2], None, MUL).then_inc(sem["mix_ready"], 1)
                dve.wait_ge(sem["mix_ready"], c.done("mix_ready"))

            def mix(g, b):
                dve.wait_ge(sem["full7"], c.done("full7"))
                v.tensor_copy(oS[:, :, b * NQ:(b + 1) * NQ], bank[7][:, 0:32].rearrange("p (k q) -> p k q", k=4)
                              ).then_inc(sem["drained7"], 1)
                dve.wait_ge(sem["drained7"], c.done("drained7"))

            def sample_end(g):
                dve.wait_ge(sem["gs_out"], c.before("gs_out"))
                v.tensor_tensor(oQ[:], oS[:], oS[:], MUL).then_inc(sem["sq_ready"], 1)
                dve.wait_ge(sem["sq_ready"], c.done("sq_ready"))
                dve.wait_ge(sem["full7"], c.done("full7"))
                o.link(v.tensor_reduce(rsS[:].rearrange("p (h q) -> p h q", h=2),
                                       bank[7][:, 0:256].rearrange("p (h e q) -> p h q e", h=2, e=2), AX.X, ADD))
                variance(rsS[:], 256).then_inc(sem["drained7"], 1)
                dve.wait_ge(sem["drained7"], c.done("drained7"))
                dve.wait_ge(sem["s_rstd"], c.done("s_rstd"))
                o4 = oS[:].rearrange("p (h e) q -> p h e q", h=2)
                o.link(v.tensor_tensor(o4, o4, rsS[:].rearrange("p (h o q) -> p h o q", h=2, o=1).broadcast_to([128, 2, 2, SMP]), MUL))
                for e in range(2):
                    view = lambda a: a[:].rearrange("p (h e) q -> p h e q", h=2)[:, :, e, :]
                    ins = v.scalar_tensor_tensor(out=view(oQ), in0=view(oS), scalar=subln[:, e:e + 1], in1=view(sgS), op0=MUL, op1=MUL)
                    if e:
                        ins.then_inc(sem["gs_ready"], 1)
                        dve.wait_ge(sem["gs_ready"], c.done("gs_ready"))
                    else:
                        o.link(ins)

            def carry(g):
                for n in ("proj0_drained", "proj1_drained", "drained7", "full6", "full7"):
                    dve.wait_ge(sem[n], c.before(n))
                for hh in range(2):
                    o.link(v.tensor_copy(qS[:, 2 * hh:2 * hh + 2, :], qT[hh][:, :, SEQ:T]))
                    o.link(v.tensor_copy(kS[:, 2 * hh:2 * hh + 2, :], kT[hh][:, :, SEQ:T]))
                    o.link(v.tensor_copy(vS[0:SMP, hh * 256:hh * 256 + 256], vn[hh][0:SMP, 4, :]))
                v.tensor_copy(sgS[:], sgN[:]).then_inc(sem["carried"], 1)
                dve.wait_ge(sem["carried"], c.done("carried"))

            def load_rope(g):
                o.link(v.memset(qz[:], 0.0))

            def rope_(g, which):
                for n in ("proj0_drained", "proj1_drained"):
                    dve.wait_ge(sem[n], c.before(n))
                dve.wait_ge(rope_in, 16)
                for n in ("full4", "full5"):
                    dve.wait_ge(sem[n], c.before(n))
                dst = (rqT, rkT)[which]
                cos, sin = rope[:, 0:T], rope[:, T:2 * T]
                o.link(v.tensor_tensor(dst[:, 0, :], raw[:, 0, :], cos, MUL))
                o.link(v.tensor_tensor(rt[:, 0, :], raw[:, 1, :], sin, MUL))
                o.link(v.tensor_tensor(dst[:, 0, :], dst[:, 0, :], rt[:, 0, :], SUB))
                o.link(v.tensor_tensor(dst[:, 1, :], raw[:, 0, :], sin, MUL))
                o.link(v.tensor_tensor(rt[:, 1, :], raw[:, 1, :], cos, MUL))
                v.tensor_tensor(dst[:, 1, :], dst[:, 1, :], rt[:, 1, :], ADD).then_inc(sem["rotated"], 1)
                dve.wait_ge(sem["rotated"], c.done("rotated"))

            def ret_scores(g, c_):
                lo = c_ * 128
                dve.wait_ge(sem["head_in"], c.before("head_in"))
                dve.wait_ge(sem["full6"], c.before("full6"))
                dve.wait_ge(sem["full4"], c.done("full4"))
                v.tensor_tensor(sT[:], bank[4][:, 0:128], hc[:, 0:128], MUL).then_inc(sem["drained4"], 1)
                dve.wait_ge(sem["drained4"], c.done("drained4"))
                for e in range(2):
                    ins = v.tensor_tensor(qd[:, e, :], rqT[:, e, lo:lo + 128], hc[:, 128:256], MUL)
                    if e:
                        ins.then_inc(sem["qd_ready"], 1)
                        dve.wait_ge(sem["qd_ready"], c.done("qd_ready"))
                    else:
                        o.link(ins)

            def ret_state(g, c_):
                dve.wait_ge(sem["full6"], c.before("full6"))
                dve.wait_ge(sem["sp_out"], c.before("sp_out"))
                for e in range(2):
                    dve.wait_ge(sem[f"full{4 + e}"], c.done(f"full{4 + e}"))
                    if c_:
                        ins = v.scalar_tensor_tensor(out=Sp[:, e, :], in0=Sp[:, e, :], scalar=hc[:, 393:394], in1=bank[4 + e][:, :],
                                                     op0=MUL, op1=ADD)
                    else:
                        ins = v.tensor_copy(Sp[:, e, :], bank[4 + e][:, :])
                    ins.then_inc(sem[f"drained{4 + e}"], 1)
                    dve.wait_ge(sem[f"drained{4 + e}"], c.done(f"drained{4 + e}"))

            def ret_norm(g, t):
                R = TILES[t][1]
                dve.wait_ge(sem["drained6"], c.before("drained6"))
                o.link(v.tensor_tensor_reduce(out=rjunk[0:R, :], in0=oN[0:R, t, :], in1=oN[0:R, t, :], scale=1.0, scalar=0.0,
                                              op0=MUL, op1=ADD, accum_out=rst[0:R, 0:1]))
                variance(rst[0:R, 0:1], 512).then_inc(sem["o_var"], 1)
                dve.wait_ge(sem["o_var"], c.done("o_var"))
                dve.wait_ge(sem["o_rstd"], c.done("o_rstd"))
                v.tensor_scalar(oN[0:R, t, :], oN[0:R, t, :], rst[0:R, 1:2], None, MUL).then_inc(sem["o_normed"], 1)
                dve.wait_ge(sem["o_normed"], c.done("o_normed"))

            def rs_scores(g):
                dve.wait_ge(sem["full6"], c.before("full6"))
                dve.wait_ge(sem["full4"], c.done("full4"))
                v.tensor_tensor(sT[0:SMP, 0:SMP], bank[4][0:SMP, 0:SMP], hc[0:SMP, 320:384], MUL).then_inc(sem["drained4"], 1)
                dve.wait_ge(sem["drained4"], c.done("drained4"))
                for e in range(2):
                    o.link(v.tensor_tensor(qz[:, e, :].rearrange("p (b r) -> p b r", r=72)[:, :, 0:8],
                                           rqT[:, e, SEQ:T].rearrange("p (b i) -> p b i", i=8),
                                           hc[:, 256:320].rearrange("p (b i) -> p b i", i=8), MUL))
                dve.wait_ge(sem["full5"], c.done("full5"))
                for b in range(NB):
                    ins = v.tensor_scalar(kz[:, b, :], bank[5][0:SMP, 0:256], hc[0:SMP, 384 + b:385 + b], None, MUL)
                    if b == NB - 1:
                        ins.then_inc(sem["qd_ready"], 1)
                        dve.wait_ge(sem["qd_ready"], c.done("qd_ready"))
                    else:
                        o.link(ins)
                dve.nop().then_inc(sem["drained5"], 1)

            def rs_state(g, b):
                dve.wait_ge(sem[f"state_out{b % 2}"], c.before(f"state_out{b % 2}"))
                for e in range(2):
                    dve.wait_ge(sem[f"full{4 + e}"], c.done(f"full{4 + e}"))
                    cols = slice(e * 512, (e + 1) * 512)
                    v.scalar_tensor_tensor(out=Sout[:, b % 2, cols], in0=Sin[:, b % 3, cols], scalar=hc[:, 394:395],
                                           in1=bank[4 + e][:, :], op0=MUL, op1=ADD).then_inc(sem[f"drained{4 + e}"], 1)
                    dve.wait_ge(sem[f"drained{4 + e}"], c.done(f"drained{4 + e}"))

            def gate(g, t):
                n, R = 4 + t % 2, TILES[t][1]
                for m in ("proj0_drained", "proj1_drained", f"gt_out{t % 2}"):
                    dve.wait_ge(sem[m], c.before(m))
                dve.wait_ge(sem[f"full{n}"], c.done(f"full{n}"))
                v.tensor_tensor(gt[:, t % 2, :].rearrange("p (k t) -> p k t", k=4)[:, :, 0:R],
                                bank[n][:, :].rearrange("p (k t) -> p k t", k=4)[:, :, 0:R],
                                rsg[:, :, t * 128:t * 128 + R], MUL).then_inc(sem[f"drained{n}"], 1)
                dve.wait_ge(sem[f"drained{n}"], c.done(f"drained{n}"))

            def y_tile(g, t, stage):
                R = TILES[t][1]
                n, xv, yv = nst[0:R, t % 2, :], xt[0:R, t % 2, :], yn[0:R, t % 2, :]
                dve.wait_ge(sem["y_sq"], c.done("y_sq"))
                variance(n[:, 0:1], D).then_inc(sem["y_var"], 1)
                dve.wait_ge(wpost_in, 16 * stage)
                dve.wait_ge(sem["y_rstd"], c.done("y_rstd"))
                v.scalar_tensor_tensor(out=yv, in0=low[0:R, :, :].rearrange("p a b -> p (a b)"), scalar=n[:, 1:2],
                                       in1=wpost[0:R, :], op0=MUL, op1=MUL).then_inc(sem["y_used"], 1)
                dve.wait_ge(sem["y_used"], c.done("y_used"))
                dve.wait_ge(sem[f"x_in{t % 2}"], c.done(f"x_in{t % 2}"))
                v.tensor_tensor(xv, xv, yv, ADD).then_inc(sem["x_sum"], 1)
                dve.wait_ge(sem["x_sum"], c.done("x_sum"))

            def x_tile(g, t, stage):
                R = TILES[t][1]
                dve.wait_ge(sem["x_sq"], c.done("x_sq"))
                variance(nst[0:R, t % 2, 2:3], D).then_inc(sem["x_var"], 1)
                for j in range(KT):
                    if j % 4 == 0:
                        dve.wait_ge(sem["x_hi"], c.done("x_hi") - 3 + j // 4)
                    xc = slice(t * 128, t * 128 + R)
                    last = v.scalar_tensor_tensor(out=XL[:, j, xc], in0=bank[4 + j // 4][:, (j % 4) * 128:(j % 4) * 128 + R],
                                                  scalar=wpre[:, stage, j:j + 1], in1=XH[:, j, xc].bitcast(f32), op0=MUL, op1=SUB)
                last.then_inc(sem["x_lo"], 1)
                dve.wait_ge(sem["x_lo"], c.done("x_lo"))

            run(dve, c, o, dict(row_tables=row_tables, relay_area=all_done(dve, c), split_w=split_w, split_g=split_g, evacuate=evacuate, scores=scores, pv=pv, o_transpose=o_transpose,
                                page=page, place_q=place_q, qk=qk, soft_new=soft_new, soft_exp=soft_exp,
                                e_transpose=e_transpose, mix=mix, sample_end=sample_end, carry=carry, rope=rope_, load_rope=load_rope,
                                ret_scores=lambda g, c: ret_scores(g, c), ret_state=lambda g, c: ret_state(g, c),
                                ret_norm=ret_norm, rs_scores=rs_scores, rs_state=rs_state, gate=gate, y_tile=y_tile, x_tile=x_tile))

        @block.gpsimd
        def _(pool):
            c = Count()

            begin(pool, POOL_NAMES)
            pool.nop().then_inc(starts_done, 1)
            pool.wait_ge(starts_done, 5)
            pool.wait_ge(setup_done, 2)
            pool.wait_ge(lam_dot, 1)

            def rsqrt(out, a, name, R=128, n=1):
                nc.gpsimd.tensor_tensor(out, a, power[0:R, 0:n], ALU.pow).then_inc(sem[name], 1)

            def pv(g, hp, qb, back):
                pool.wait_ge(sem["o_var"], c.done("o_var"))
                rsqrt(pst[:, 7:8], pst[:, 6:7], "o_rstd")

            def sample_end(g):
                pool.wait_ge(sem["drained7"], c.done("drained7"))
                rsqrt(rsS[:], rsS[:], "s_rstd", n=128)

            def ret_norm(g, t):
                R = TILES[t][1]
                pool.wait_ge(sem["o_var"], c.done("o_var"))
                rsqrt(rst[0:R, 1:2], rst[0:R, 0:1], "o_rstd", R)

            def y_tile(g, t, stage):
                R = TILES[t][1]
                pool.wait_ge(sem["y_var"], c.done("y_var"))
                rsqrt(nst[0:R, t % 2, 1:2], nst[0:R, t % 2, 0:1], "y_rstd", R)

            def x_tile(g, t, stage):
                R = TILES[t][1]
                pool.wait_ge(sem["x_var"], c.done("x_var"))
                rsqrt(nst[0:R, t % 2, 3:4], nst[0:R, t % 2, 2:3], "x_rstd", R)

            run(pool, c, None, dict(pv=pv, sample_end=sample_end, ret_norm=ret_norm, y_tile=y_tile, x_tile=x_tile))


_INS = ["x_prompt", "x_sample", "cache_k", "cache_v", "page_table", "state_ret", "norm_pre_attn", "w_in_attn",
        "lambda_q1", "lambda_k1", "lambda_q2", "lambda_k2", "subln_w_attn", "w_out_attn", "norm_post_attn",
        "norm_pre_ret", "w_in_ret", "w_out_ret", "norm_post_ret"]
_OUTS = [(1, SEQ, D), (NB, NQ, D), (1, SEQ, HEADS, 256), (1, SEQ, HEADS, 256), (1, HEADS, 256, 512),
         (NB, NQ, HEADS, 256), (NB, NQ, HEADS, 256), (NB, HEADS, 256, 512)]


def kernel(**inputs):
    import numpy as _np
    import concourse.bacc as _bacc
    from concourse import mybir as _mybir
    from concourse.bass_utils import run_bass_kernel_spmd as _run

    nc = _bacc.Bacc("TRN2", target_bir_lowering=False, num_devices=1)
    arrays, args = {}, []
    for name in _INS:
        a = _np.ascontiguousarray(inputs[name])
        arrays[f"in_{name}"] = a
        args.append(nc.dram_tensor(f"in_{name}", a.shape, _mybir.dt.from_np(a.dtype), kind="ExternalInput").ap())
    for i, shape in enumerate(_OUTS):
        args.append(nc.dram_tensor(f"out_{i}", shape, _mybir.dt.float32, kind="ExternalOutput").ap())
    hybrid_step_kernel(nc, *args)
    r = _run(nc, [arrays], core_ids=[0])
    return tuple(r.results[0][f"out_{i}"] for i in range(len(_OUTS)))
```
